# Optimizing a Trainium2 kernel written in Bass

```python
import jax
import jax.numpy as jnp
from jax import lax
import numpy as np

D_MODEL = 1024
BATCH = 1
SEQ = 512
DEPTH = 2

GRID_W = 64
CTX_LEN = 256
HEAD_DIM = 64
N_GROUPS = 4
MIX_WIDTH = D_MODEL
GROUP_WIDTH = MIX_WIDTH // N_GROUPS
GROUP_HEADS = GROUP_WIDTH // HEAD_DIM
Q_BLOCK = 128
ROPE_THETA = 10000.0
NORM_EPS = 1e-6
NEG_INF = -1e30
GQA_KV_HEADS = 2
MLA_Q_RANK = D_MODEL // 4
MLA_KV_RANK = D_MODEL // 8
MLA_NOPE_DIM = 64
MLA_ROPE_DIM = 32
MLA_V_DIM = GROUP_WIDTH // GROUP_HEADS
RWKV_DECAY_LORA = 64
RWKV_ICLR_LORA = 64
RWKV_GATE_LORA = 160
RWKV_GN_EPS = 64e-5
SWA_KV_HEADS = 2
WINDOW = 128
D_FF = 4 * D_MODEL

A_COLS = GROUP_WIDTH + 2 * GQA_KV_HEADS * HEAD_DIM
B_COLS = MLA_Q_RANK + MLA_KV_RANK + MLA_ROPE_DIM
C_COLS = 3 * GROUP_WIDTH + RWKV_DECAY_LORA + RWKV_ICLR_LORA + RWKV_GATE_LORA
D_COLS = GROUP_WIDTH + 2 * SWA_KV_HEADS * HEAD_DIM
IN_COLS = A_COLS + B_COLS + C_COLS + D_COLS
IN_CUTS = (A_COLS, A_COLS + B_COLS, A_COLS + B_COLS + C_COLS)
RWKV_CUTS = (GROUP_WIDTH, 2 * GROUP_WIDTH, 3 * GROUP_WIDTH,
             3 * GROUP_WIDTH + RWKV_DECAY_LORA,
             3 * GROUP_WIDTH + RWKV_DECAY_LORA + RWKV_ICLR_LORA)

kernel_name = 'hybrid_parallel_group_flow_block'

def rms_norm(x, g):
    xf = x.astype(jnp.float32)
    y = xf * lax.rsqrt(jnp.mean(xf * xf, axis=-1, keepdims=True) + NORM_EPS)
    return (y * g.astype(jnp.float32)).astype(x.dtype)

def rope_tables(row, col, rot_dim):
    n = rot_dim // 4
    inv = ROPE_THETA ** (-jnp.arange(n, dtype=jnp.float32) / n)
    ar = row[:, None] * inv
    ac = col[:, None] * inv
    return (jnp.cos(ar), jnp.sin(ar), jnp.cos(ac), jnp.sin(ac))

def _rotate(x, cos, sin):
    shape = (cos.shape[0],) + (1,) * (x.ndim - 3) + (cos.shape[1],)
    cs, sn = cos.reshape(shape), sin.reshape(shape)
    x1, x2 = jnp.split(x, 2, axis=-1)
    return jnp.concatenate([x1 * cs - x2 * sn, x1 * sn + x2 * cs], axis=-1)

def axial_rope(x, rope):
    cos_r, sin_r, cos_c, sin_c = rope
    xf = x.astype(jnp.float32)
    half = x.shape[-1] // 2
    out = jnp.concatenate([_rotate(xf[..., :half], cos_r, sin_r),
                           _rotate(xf[..., half:], cos_c, sin_c)], axis=-1)
    return out.astype(x.dtype)

def softmax_attend(q, k, v, sink):
    s = jnp.einsum('bqgrd,bkgd->bgrqk', q, k).astype(jnp.float32) * (q.shape[-1] ** -0.5)
    if sink is None:
        p = jax.nn.softmax(s, axis=-1)
    else:
        sk = jnp.broadcast_to(sink.astype(jnp.float32)[None, :, :, None, None], s.shape[:-1] + (1,))
        p = jax.nn.softmax(jnp.concatenate([sk, s], axis=-1), axis=-1)[..., 1:]
    return jnp.einsum('bgrqk,bkgd->bqgrd', p.astype(v.dtype), v)

def blocked_attend(q, k, v):
    B, T, G, R, dk = q.shape
    nb = T // Q_BLOCK
    qb = jnp.moveaxis(q.reshape(B, nb, Q_BLOCK, G, R, dk), 1, 0)
    ob = lax.map(lambda qi: softmax_attend(qi, k, v, None), qb)
    return jnp.moveaxis(ob, 0, 1).reshape(B, T, G, R, v.shape[-1])

def banded_window_attend(q, k, v, k_ctx, v_ctx, sink):
    B, T, G, R, d = q.shape
    W = WINDOW
    nb = T // W

    def band(t):
        tp = jnp.pad(t, ((0, 0), (W, W), (0, 0), (0, 0))).reshape(B, nb + 2, W, G, t.shape[-1])
        return jnp.concatenate([tp[:, :-2], tp[:, 1:-1], tp[:, 2:]], axis=2)

    kb, vb = band(k), band(v)
    qb = q.reshape(B, nb, W, G, R, d)
    scale = d ** -0.5
    s_win = jnp.einsum('bnqgrd,bnkgd->bgrnqk', qb, kb).astype(jnp.float32) * scale
    s_ctx = jnp.einsum('bnqgrd,bcgd->bgrnqc', qb, k_ctx).astype(jnp.float32) * scale
    qpos = jnp.arange(T).reshape(nb, W)[:, :, None]
    kpos = (jnp.arange(nb)[:, None] * W - W + jnp.arange(3 * W)[None, :])[:, None, :]
    valid = (jnp.abs(qpos - kpos) <= W) & (kpos >= 0) & (kpos < T)
    s_win = jnp.where(valid, s_win, NEG_INF)
    sk = jnp.broadcast_to(sink.astype(jnp.float32)[None, :, :, None, None, None], s_win.shape[:-1] + (1,))
    p = jax.nn.softmax(jnp.concatenate([sk, s_win, s_ctx], axis=-1), axis=-1)
    p_win = p[..., 1:1 + 3 * W].astype(v.dtype)
    p_ctx = p[..., 1 + 3 * W:].astype(v.dtype)
    o = (jnp.einsum('bgrnqk,bnkgd->bnqgrd', p_win, vb)
         + jnp.einsum('bgrnqc,bcgd->bnqgrd', p_ctx, v_ctx))
    return o.reshape(B, T, G, R, d)

def split_gqa(z, n_kv):
    B, T, _ = z.shape
    q, k, v = jnp.split(z, (GROUP_WIDTH, GROUP_WIDTH + n_kv * HEAD_DIM), axis=-1)
    return (q.reshape(B, T, n_kv, GROUP_HEADS // n_kv, HEAD_DIM),
            k.reshape(B, T, n_kv, HEAD_DIM),
            v.reshape(B, T, n_kv, HEAD_DIM))

def mla_qkv(z, p, rope):
    B, T, _ = z.shape
    cq, ckv, kr = jnp.split(z, (MLA_Q_RANK, MLA_Q_RANK + MLA_KV_RANK), axis=-1)
    q = (rms_norm(cq, p['mla_q_norm']) @ p['mla_w_uq']).reshape(B, T, GROUP_HEADS, MLA_NOPE_DIM + MLA_ROPE_DIM)
    kv = (rms_norm(ckv, p['mla_kv_norm']) @ p['mla_w_ukv']).reshape(B, T, GROUP_HEADS, MLA_NOPE_DIM + MLA_V_DIM)
    q_nope, q_rope = jnp.split(q, (MLA_NOPE_DIM,), axis=-1)
    k_nope, v = jnp.split(kv, (MLA_NOPE_DIM,), axis=-1)
    kr = kr.reshape(B, T, 1, MLA_ROPE_DIM)
    if rope is not None:
        q_rope = axial_rope(q_rope, rope)
        kr = axial_rope(kr, rope)
    q = jnp.concatenate([q_nope, q_rope], axis=-1)[:, :, :, None, :]
    k = jnp.concatenate([k_nope, jnp.broadcast_to(kr, (B, T, GROUP_HEADS, MLA_ROPE_DIM))], axis=-1)
    return q, k, v

def token_shift_centred(z, mu):
    zp = jnp.pad(z, ((0, 0), (1, 1), (0, 0)))
    return z + mu * (0.5 * (zp[:, :-2] + zp[:, 2:]) - z)

def rwkv_prepare(z, p):
    z = token_shift_centred(z, p['rwkv_mu'])
    r, k, v, wl, al, gl = jnp.split(z, RWKV_CUTS, axis=-1)
    B, T, _ = z.shape

    def heads(t):
        return t.reshape(B, T, GROUP_HEADS, HEAD_DIM).astype(jnp.float32)

    wt = jnp.tanh(wl)
    dirs = []
    for d in range(2):
        w_log = -jax.nn.softplus(-(p['rwkv_w0'][d] + wt @ p['rwkv_w2'][d])) - 0.5
        decay = jnp.exp(-jnp.exp(w_log.astype(jnp.float32)))
        a = jax.nn.sigmoid(p['rwkv_a0'][d] + al @ p['rwkv_a2'][d])
        kk = heads(k * p['rwkv_k_k'][d])
        kk = kk / jnp.maximum(jnp.sqrt(jnp.sum(kk * kk, axis=-1, keepdims=True)), 1e-12)
        kd = heads(k * (1.0 + (a - 1.0) * p['rwkv_k_a'][d]))
        dirs.append((heads(decay), kd, -kk, kk * heads(a)))
    return heads(r), heads(v), gl, dirs

def rwkv_scan(S0, r, w, k, v, a, b, reverse):
    def step(S, inp):
        r_t, w_t, k_t, v_t, a_t, b_t = inp
        sa = jnp.einsum('bhij,bhj->bhi', S, a_t)
        S = S * w_t[:, :, None, :] + sa[..., :, None] * b_t[:, :, None, :] + v_t[..., :, None] * k_t[:, :, None, :]
        return S, jnp.einsum('bhij,bhj->bhi', S, r_t)

    xs = tuple(jnp.moveaxis(t, 1, 0) for t in (r, w, k, v, a, b))
    S, ys = lax.scan(step, S0, xs, reverse=reverse)
    return S, jnp.moveaxis(ys, 0, 1)

def rwkv_output(y, r, v, dirs, gl, p, dtype):
    B, T, H, N = y.shape
    mean = jnp.mean(y, axis=-1, keepdims=True)
    var = jnp.mean(jnp.square(y - mean), axis=-1, keepdims=True)
    yn = ((y - mean) * lax.rsqrt(var + RWKV_GN_EPS)).reshape(B, T, H * N)
    yn = yn * p['rwkv_ln_w'].astype(jnp.float32) + p['rwkv_ln_b'].astype(jnp.float32)
    r_k = p['rwkv_r_k'].astype(jnp.float32)
    bonus = ((jnp.sum(r * dirs[0][1] * r_k, axis=-1, keepdims=True)
              + jnp.sum(r * dirs[1][1] * r_k, axis=-1, keepdims=True)) * v).reshape(B, T, H * N)
    g = (jax.nn.sigmoid(gl) @ p['rwkv_g2']).astype(jnp.float32)
    return ((yn + bonus) * g).astype(dtype)

def rwkv_mix(zr, zrc, p, with_ctx_out):
    r_c, v_c, gl_c, dirs_c = rwkv_prepare(zrc, p)
    r_l, v_l, gl_l, dirs_l = rwkv_prepare(zr, p)
    S0 = jnp.zeros((zr.shape[0], GROUP_HEADS, HEAD_DIM, HEAD_DIM), jnp.float32)
    ys_c, ys_l = [], []
    for d, rev in enumerate((False, True)):
        w_c, k_c, a_c, b_c = dirs_c[d]
        S_ctx, y_c = rwkv_scan(S0, r_c, w_c, k_c, v_c, a_c, b_c, rev)
        w_l, k_l, a_l, b_l = dirs_l[d]
        _, y_l = rwkv_scan(S_ctx, r_l, w_l, k_l, v_l, a_l, b_l, rev)
        ys_c.append(y_c)
        ys_l.append(y_l)
    out = rwkv_output(ys_l[0] + ys_l[1], r_l, v_l, dirs_l, gl_l, p, zr.dtype)
    out_c = rwkv_output(ys_c[0] + ys_c[1], r_c, v_c, dirs_c, gl_c, p, zrc.dtype) if with_ctx_out else None
    return out, out_c

def merge_groups(outs):
    return jnp.concatenate([o.reshape(o.shape[0], o.shape[1], -1) for o in outs], axis=-1)

def token_mixer(h, hc, p, rope_hd, rope_mla, with_ctx_out):
    za, zb, zr, zd = jnp.split(h @ p['w_in'], IN_CUTS, axis=-1)
    zac, zbc, zrc, zdc = jnp.split(hc @ p['w_in'], IN_CUTS, axis=-1)
    outs, outs_c = [], []
    q, k, v = split_gqa(za, GQA_KV_HEADS)
    qc, kc, vc = split_gqa(zac, GQA_KV_HEADS)
    q = axial_rope(rms_norm(q, p['gqa_q_norm']), rope_hd)
    k = axial_rope(rms_norm(k, p['gqa_k_norm']), rope_hd)
    qc = rms_norm(qc, p['gqa_q_norm'])
    kc = rms_norm(kc, p['gqa_k_norm'])
    outs.append(blocked_attend(q, jnp.concatenate([k, kc], axis=1), jnp.concatenate([v, vc], axis=1)))
    if with_ctx_out:
        outs_c.append(softmax_attend(qc, kc, vc, None))
    q, k, v = mla_qkv(zb, p, rope_mla)
    qc, kc, vc = mla_qkv(zbc, p, None)
    outs.append(blocked_attend(q, jnp.concatenate([k, kc], axis=1), jnp.concatenate([v, vc], axis=1)))
    if with_ctx_out:
        outs_c.append(softmax_attend(qc, kc, vc, None))
    o, oc = rwkv_mix(zr, zrc, p, with_ctx_out)
    outs.append(o)
    if with_ctx_out:
        outs_c.append(oc)
    q, k, v = split_gqa(zd, SWA_KV_HEADS)
    qc, kc, vc = split_gqa(zdc, SWA_KV_HEADS)
    q = axial_rope(q, rope_hd)
    k = axial_rope(k, rope_hd)
    sink = p['swa_sink'].reshape(SWA_KV_HEADS, GROUP_HEADS // SWA_KV_HEADS)
    outs.append(banded_window_attend(q, k, v, kc, vc, sink))
    if with_ctx_out:
        outs_c.append(softmax_attend(qc, kc, vc, sink))
    y = merge_groups(outs) @ p['w_out']
    yc = merge_groups(outs_c) @ p['w_out'] if with_ctx_out else None
    return y, yc

def sq_relu_mlp(h, w1, w2):
    return jnp.square(jax.nn.relu(h @ w1)) @ w2

def setup_inputs(seed: int = 0) -> dict:
    key = jax.random.key(seed)
    keys = iter(jax.random.split(key, 40))

    def nrm(shape, scale):
        return jax.random.normal(next(keys), shape, jnp.float32) * scale

    def gain(shape):
        return 1.0 + nrm(shape, 0.02)

    def unif(shape, lo, hi):
        return jax.random.uniform(next(keys), shape, jnp.float32, lo, hi)

    L, D, H, N, GW = DEPTH, D_MODEL, GROUP_HEADS, HEAD_DIM, GROUP_WIDTH
    return {
        'x': nrm((BATCH, SEQ, D), 1.0),
        'c': nrm((BATCH, D), 1.0),
        'ctx': nrm((BATCH, CTX_LEN, D), 1.0),
        'c_ctx': nrm((D,), 1.0),
        'w_mod': nrm((L, D, 6 * D), 0.5 * D ** -0.5),
        'b_mod': nrm((L, 6 * D), 0.02),
        'g_pre_mix': gain((L, D)),
        'g_post_mix': gain((L, D)),
        'g_pre_mlp': gain((L, D)),
        'g_post_mlp': gain((L, D)),
        'w_in': nrm((L, D, IN_COLS), D ** -0.5),
        'gqa_q_norm': gain((L, N)),
        'gqa_k_norm': gain((L, N)),
        'mla_q_norm': gain((L, MLA_Q_RANK)),
        'mla_kv_norm': gain((L, MLA_KV_RANK)),
        'mla_w_uq': nrm((L, MLA_Q_RANK, H * (MLA_NOPE_DIM + MLA_ROPE_DIM)), MLA_Q_RANK ** -0.5),
        'mla_w_ukv': nrm((L, MLA_KV_RANK, H * (MLA_NOPE_DIM + MLA_V_DIM)), MLA_KV_RANK ** -0.5),
        'rwkv_mu': unif((L, C_COLS), 0.0, 1.0),
        'rwkv_w0': unif((L, 2, GW), -6.0, -1.0),
        'rwkv_w2': nrm((L, 2, RWKV_DECAY_LORA, GW), 0.1 * RWKV_DECAY_LORA ** -0.5),
        'rwkv_a0': nrm((L, 2, GW), 0.1),
        'rwkv_a2': nrm((L, 2, RWKV_ICLR_LORA, GW), 0.5 * RWKV_ICLR_LORA ** -0.5),
        'rwkv_k_k': 0.85 + nrm((L, 2, GW), 0.05),
        'rwkv_k_a': 1.0 + nrm((L, 2, GW), 0.05),
        'rwkv_r_k': nrm((L, H, N), 0.1),
        'rwkv_g2': nrm((L, RWKV_GATE_LORA, GW), RWKV_GATE_LORA ** -0.5),
        'rwkv_ln_w': gain((L, GW)),
        'rwkv_ln_b': nrm((L, GW), 0.02),
        'swa_sink': nrm((L, H), 0.5),
        'w_out': nrm((L, MIX_WIDTH, D), MIX_WIDTH ** -0.5),
        'w_mlp1': nrm((L, D, D_FF), D ** -0.5),
        'w_mlp2': nrm((L, D_FF, D), D_FF ** -0.5),
    }

def reference(x, c, ctx, c_ctx, w_mod, b_mod, g_pre_mix, g_post_mix, g_pre_mlp, g_post_mlp, w_in,
              gqa_q_norm, gqa_k_norm, mla_q_norm, mla_kv_norm, mla_w_uq, mla_w_ukv,
              rwkv_mu, rwkv_w0, rwkv_w2, rwkv_a0, rwkv_a2, rwkv_k_k, rwkv_k_a, rwkv_r_k, rwkv_g2,
              rwkv_ln_w, rwkv_ln_b, swa_sink, w_out, w_mlp1, w_mlp2):
    T = x.shape[1]
    ROWS = T // GRID_W
    row = jnp.broadcast_to(jnp.arange(ROWS, dtype=jnp.float32)[:, None], (ROWS, GRID_W)).reshape(-1)
    col = jnp.broadcast_to(jnp.arange(GRID_W, dtype=jnp.float32)[None, :], (ROWS, GRID_W)).reshape(-1)
    rope_hd = rope_tables(row, col, HEAD_DIM)
    rope_mla = rope_tables(row, col, MLA_ROPE_DIM)
    silu_c = jax.nn.silu(c)
    silu_cc = jax.nn.silu(c_ctx)[None, :]
    xc = ctx
    for l in range(DEPTH):
        last = l == DEPTH - 1
        m = (silu_c @ w_mod[l] + b_mod[l])[:, None, :]
        mc = (silu_cc @ w_mod[l] + b_mod[l])[:, None, :]
        sh1, sc1, gt1, sh2, sc2, gt2 = jnp.split(m, 6, axis=-1)
        sh1c, sc1c, gt1c, sh2c, sc2c, gt2c = jnp.split(mc, 6, axis=-1)
        p = {
            'w_in': w_in[l], 'w_out': w_out[l],
            'gqa_q_norm': gqa_q_norm[l], 'gqa_k_norm': gqa_k_norm[l],
            'mla_q_norm': mla_q_norm[l], 'mla_kv_norm': mla_kv_norm[l],
            'mla_w_uq': mla_w_uq[l], 'mla_w_ukv': mla_w_ukv[l],
            'rwkv_mu': rwkv_mu[l], 'rwkv_w0': rwkv_w0[l], 'rwkv_w2': rwkv_w2[l],
            'rwkv_a0': rwkv_a0[l], 'rwkv_a2': rwkv_a2[l], 'rwkv_k_k': rwkv_k_k[l],
            'rwkv_k_a': rwkv_k_a[l], 'rwkv_r_k': rwkv_r_k[l], 'rwkv_g2': rwkv_g2[l],
            'rwkv_ln_w': rwkv_ln_w[l], 'rwkv_ln_b': rwkv_ln_b[l], 'swa_sink': swa_sink[l],
        }
        h = rms_norm(x, g_pre_mix[l]) * (1.0 + sc1) + sh1
        hc = rms_norm(xc, g_pre_mix[l]) * (1.0 + sc1c) + sh1c
        y, yc = token_mixer(h, hc, p, rope_hd, rope_mla, not last)
        x = x + gt1 * rms_norm(y, g_post_mix[l])
        h = rms_norm(x, g_pre_mlp[l]) * (1.0 + sc2) + sh2
        x = x + gt2 * rms_norm(sq_relu_mlp(h, w_mlp1[l], w_mlp2[l]), g_post_mlp[l])
        if not last:
            xc = xc + gt1c * rms_norm(yc, g_post_mix[l])
            hc = rms_norm(xc, g_pre_mlp[l]) * (1.0 + sc2c) + sh2c
            xc = xc + gt2c * rms_norm(sq_relu_mlp(hc, w_mlp1[l], w_mlp2[l]), g_post_mlp[l])
    return x


_drawn_inputs = setup_inputs


def setup_inputs(seed=0):
    import zlib

    import numpy as np

    out = dict(_drawn_inputs(seed))
    spreads = {}
    factors = {'g_pre_mix': 4.904,
     'g_post_mix': 6.777,
     'g_pre_mlp': 6.418,
     'g_post_mlp': 7.052,
     'gqa_q_norm': 8.0,
     'gqa_k_norm': 8.0,
     'mla_q_norm': 8.0,
     'mla_kv_norm': 8.0,
     'rwkv_w2': 8.0,
     'rwkv_a0': 5.189,
     'rwkv_ln_w': 41.991,
     'rwkv_ln_b': 37.015,
     'swa_sink': 8.0}
    for name, (base, spread) in spreads.items():
        noise = np.random.default_rng([zlib.crc32(name.encode()), seed]).standard_normal(out[name].shape)
        drawn = base * np.exp(spread * noise) if base else spread * noise
        out[name] = jnp.asarray(drawn.astype(out[name].dtype))
    for name, factor in factors.items():
        out[name] = (out[name] * factor).astype(out[name].dtype)
    return out
```

```python
from contextlib import ExitStack

import concourse.bass as bass
from concourse import mybir
import numpy as np

ALU = mybir.AluOpType
ACT = mybir.ActivationFunctionType
AX = mybir.AxisListType
F32 = mybir.dt.float32
BF16 = mybir.dt.bfloat16
ds = bass.ds

P = 128
DM = 1024
KT = DM // P
LAT = 512
CTX = 256
TOK = LAT + CTX
NBL, NBC = LAT // P, CTX // P
NB = NBL + NBC
DEPTH = 2
NZ = 20
NMOD = 48
SLOTS = 4
SLAB = 1024
FFG = 4
F_IN = NMOD // SLOTS
F_OUT = F_IN + NZ // SLOTS
F_MLP = F_OUT + KT // SLOTS
FILLS = F_MLP + 2 * FFG * KT // SLOTS
EPS = 1e-6
GN_EPS = 64e-5
DECAY = 0.6065306597126334
CH = 64
LEVELS = (2, 4, 8, 16, 32)
NEG = -1e30

A_Q, A_K, A_V, D_Q, D_K, D_V, C_Q, C_KV = 0, 2, 3, 4, 6, 7, 8, 10
R_R, R_K, R_V, R_WA, R_GL, R_MISC = 11, 13, 15, 17, 18, 19

PC = {}
_at = 0
for _name, _n in (("b_mod", 48), ("g_pre_mix", 8), ("g_post_mix", 8), ("g_pre_mlp", 8), ("g_post_mlp", 8),
                  ("q_norm", 1), ("k_norm", 1), ("cq_norm", 2), ("ckv_norm", 1), ("mu", 9), ("w0", 4), ("a0", 4),
                  ("k_k", 4), ("k_a", 4), ("r_k", 2), ("sink", 4)):
    PC[_name] = _at
    _at += _n
NPC = _at

K_ID, K_ONES, K_BD, K_ROT64, K_ROT96 = range(5)
NKF = 5
MASKS_DIR = 2 + 2 + len(LEVELS)
NKM = 2 * MASKS_DIR

W_QB, W_KB, W_VB, W_VA, W_VD = 0, 3072, 6144, 7680, 8448
W_ROPE, W_WMASK, W_UQ, W_UKV = 9472, 11520, 13056, 13824
W_P, W_PT, W_QT = 14336, 15872, 17408
W_U, W_KD, W_G, W_LN = 0, 0, 3072, 17920
W_SCR, SCR = 4608, 6144
W_W2A2, W_G2A, W_G2B, W_SMASK, W_SG, W_A, W_RN = 6912, 7424, 7680, 7936, 8704, 11776, 14848
W_ST = W_SCR + 2 * SCR
WORK = 18432


def backbone(nc, xT_d, cT_d, pcol_d, constf_d, constm_d, rope_d, wmask_d, wmod_d, win_d, wout_d, w1_d, w2_d,
             uq_d, ukv_d, w2a2_d, g2_d, ln_d, smask_d, out_d):
    with ExitStack() as ctx:
        def sb(name, cols, dt=F32):
            return ctx.enter_context(nc.sbuf_tensor(name, [P, cols], dt))

        def sem(name):
            return ctx.enter_context(nc.semaphore(name))

        xT = sb("xT", KT * TOK)
        hT = sb("hT", KT * TOK)
        zT = sb("zT", NZ * TOK)
        slab = sb("slab", SLOTS * SLAB)
        work = sb("work", WORK)
        pcol = sb("pcol", DEPTH * NPC)
        kf = sb("kf", NKF * P)
        km = sb("km", NKM * P, BF16)
        cT = sb("cT", KT * 2)
        silu = sb("silu", KT * 2)
        modT = sb("modT", NMOD * 2)
        gain = sb("gain", 4 * 16)
        omm = sb("omm", 32)
        small = sb("small", 96)
        bon = sb("bon", NB * 4)
        eps = sb("eps", 1)
        ps = ctx.enter_context(nc.psum_tensor("ps", [P, 4096], F32))

        xv = xT[:, :].rearrange("p (k t) -> p k t", k=KT)
        hv = hT[:, :].rearrange("p (k t) -> p k t", k=KT)
        zv = zT[:, :].rearrange("p (k t) -> p k t", k=NZ)
        mv = modT[:, :].rearrange("p (k s) -> p k s", s=2)
        gv = gain[:, :].rearrange("p (n k s) -> p n k s", n=4, s=2)
        ident, ones, bd = (kf[:, k * P:(k + 1) * P] for k in (K_ID, K_ONES, K_BD))
        rot64 = kf[:, K_ROT64 * P:(K_ROT64 + 1) * P]
        rot96 = kf[0:96, K_ROT96 * P:K_ROT96 * P + 96]
        modrow = work[0:2, 0:NMOD * P]

        def wv(at, *dims):
            n = int(np.prod(dims))
            if len(dims) == 1:
                return work[:, at:at + n]
            if len(dims) == 2:
                return work[:, at:at + n].rearrange("p (a b) -> p a b", a=dims[0])
            return work[:, at:at + n].rearrange("p (a b c) -> p a b c", a=dims[0], b=dims[1])

        qB, kB = wv(W_QB, 4, TOK), wv(W_KB, 4, TOK)
        vB, vA = wv(W_VB, NB, 256), wv(W_VA, NB, P)
        vD = wv(W_VD, 8, P)
        rope = wv(W_ROPE, 4, LAT)
        wmask = wv(W_WMASK, NBL, 384)
        uq, ukv = wv(W_UQ, 2, 384), wv(W_UKV, 512)
        prob, probT = wv(W_P, 2, TOK), wv(W_PT, 2, TOK)
        qa, qd = (zT[:, t * TOK:t * TOK + 4 * P].rearrange("p (h t) -> p h t", h=4) for t in (C_Q, C_Q + 1))
        qb = wv(W_QT, 4, P)
        kwin = zT[:, C_KV * TOK:C_KV * TOK + 384]
        mix = hT[:, :].rearrange("p (b f) -> p b f", b=NB)
        oT = wv(0, KT, TOK)
        h1 = wv(0, KT, TOK)
        yT = zv[:, 0:KT, :]
        sq = zv[:, KT:2 * KT, :]
        rs = zv[:, NZ - 1, :]
        uS = wv(W_U, 9, TOK)
        kd, gtok = wv(W_KD, 4, TOK), wv(W_G, NB, 256)
        lnw, lnb = wv(W_LN, 256), wv(W_LN + 256, 256)
        nkk, bh, cs = zv[:, 0:4, :], zv[:, 4:8, :], zv[:, 15:19, :]
        vtok = zT[:, 8 * TOK:10 * TOK].rearrange("p (b f) -> p b f", b=NB)
        bonus_in = zv[:, R_K:R_K + 2, :]
        yrev = zT[:, R_K * TOK:(R_K + 2) * TOK].rearrange("p (b f) -> p b f", b=NB)
        w2a2, g2a, g2b = wv(W_W2A2, 512), wv(W_G2A, 256), work[0:32, W_G2B:W_G2B + 256]
        smask = wv(W_SMASK, TOK)
        sg, aa, rn = wv(W_SG, 4, TOK), wv(W_A, 4, TOK), wv(W_RN, 4, TOK)

        G = []
        for g in range(2):
            o = W_SCR + g * SCR
            G.append(dict(
                ar=wv(o, 4, 2, P),
                bt=wv(o + 1024, 2, P), kt=wv(o + 1280, 2, P), ei=wv(o + 1536, 2, P),
                x=wv(o + 1024, 4, P),
                uv=wv(o + 1024, 4, 64),
                akv=wv(o + 1536, 4, 64),
                ep=sb(f"decay{g}", 260)[:, :].rearrange("p (f c t) -> p f c t", f=2, c=2),
                tok=wv(o + 1792, 1024),
                vs=wv(o + 2816, 256), abr=wv(o + 3072, 4, 256), akr=wv(o + 4096, 4, 256),
                t=wv(o + 5120, 4, P), tt=wv(o + 5632, 4, P),
                wt=wv(o + 5120, 4, P)))
        for g in range(2):
            G[g]["u"] = zT[:, 10 * TOK + g * 256:10 * TOK + g * 256 + 256].rearrange("p (h i) -> p h i", h=4)
        st = [wv(W_ST + g * 256, 2, 2, 64) for g in range(2)]
        s1 = [wv(W_ST + 512 + g * P, 2, 64) for g in range(2)]

        def mask(g, k, n=1):
            o = (g * MASKS_DIR + k) * P
            return km[:, o:o + n * P]

        s_const = sem("s_const")
        s_x = sem("s_x")
        s_maskraw = sem("s_maskraw")
        s_masks = sem("s_masks")
        s_slab = [sem(f"s_slab{q}") for q in range(SLOTS)]
        s_tile = [sem(f"s_tile{q}") for q in range(SLOTS)]
        s_silu = sem("s_silu")
        s_modps = sem("s_modps")
        s_modrow = sem("s_modrow")
        s_modT = sem("s_modT")
        s_gain = sem("s_gain")
        s_sq = sem("s_sq")
        s_ssq = sem("s_ssq")
        s_ms = sem("s_ms")
        s_rt = sem("s_rt")
        s_xn = sem("s_xn")
        s_h = sem("s_h")
        s_xup = sem("s_xup")
        s_ev = sem("s_ev")
        s_ev2 = sem("s_ev2")
        s_h1 = sem("s_h1")
        s_dve = sem("s_dve")
        s_pool = sem("s_pool")
        s_atab = sem("s_atab")
        s_psq = sem("s_psq")
        s_pss = sem("s_pss")
        s_prt = sem("s_prt")
        s_pn = sem("s_pn")
        s_pair = sem("s_pair")
        s_paire = sem("s_paire")
        s_rot = sem("s_rot")
        s_cosd = sem("s_cosd")
        s_roped = sem("s_roped")
        s_pads = sem("s_pads")
        s_krc = sem("s_krc")
        s_qt = sem("s_qt")
        s_qz = sem("s_qz")
        s_kw = sem("s_kw")
        s_S = sem("s_S")
        s_nm = sem("s_nm")
        s_P = sem("s_P")
        s_es = sem("s_es")
        s_T = sem("s_T")
        s_pta = sem("s_pta")
        s_ptd = sem("s_ptd")
        s_O = sem("s_O")
        s_on = sem("s_on")
        s_rtab = sem("s_rtab")
        s_ln = sem("s_ln")
        s_ush = sem("s_ush")
        s_zs = sem("s_zs")
        s_shift = sem("s_shift")
        s_gate = sem("s_gate")
        s_rp = sem("s_rp")
        s_rpe = sem("s_rpe")
        s_kk = sem("s_kk")
        s_kkq = sem("s_kkq")
        s_kks = sem("s_kks")
        s_kkr = sem("s_kkr")
        s_prep = sem("s_prep")
        s_bonin = sem("s_bonin")
        s_bonps = sem("s_bonps")
        s_bon = sem("s_bon")

        def pair(name):
            return [sem(f"{name}{g}") for g in range(2)]

        s_E, s_AR, s_BK, s_V = pair("s_E"), pair("s_AR"), pair("s_BK"), pair("s_V")
        s_pre, s_msk, s_tti, s_tok = pair("s_pre"), pair("s_msk"), pair("s_tti"), pair("s_tok")
        s_X, s_Xm, s_Tp, s_Tu = pair("s_X"), pair("s_Xm"), pair("s_Tp"), pair("s_Tu")
        s_W, s_Wt, s_kv, s_kve = pair("s_W"), pair("s_Wt"), pair("s_kv"), pair("s_kve")
        s_U, s_Us, s_dS, s_Sn, s_y, s_ye = pair("s_U"), pair("s_Us"), pair("s_dS"), pair("s_Sn"), pair("s_y"), pair("s_ye")
        s_seen = sem("s_seen")
        s_rout = sem("s_rout")
        s_ot = sem("s_ot")
        s_ote = sem("s_ote")
        s_out = sem("s_out")

        def streams(l):
            return ((NBL, 0), (NBC, NBL)) if l < DEPTH - 1 else ((NBL, 0),)

        SCAN = ((NBC, NBL), (NBL, 0))

        def segs(l, mixed):
            if l == DEPTH - 1 and mixed:
                return ((0, 0, LAT),)
            return ((0, 0, LAT), (1, LAT, TOK))

        class Chain:

            def __init__(self, eng, s):
                self.eng, self.s, self.n, self.i, self.per, self.mark = eng, s, 0, None, 0, 0

            def link(self, ins):
                ins.then_inc(self.s, 1)
                self.n += 1
                if self.i is None:
                    self.eng.wait_ge(self.s, self.n)
                else:
                    self.eng.wait_ge(self.s, self.i * self.per + self.n)

            def enter(self, i, per):
                self.i, self.per, self.mark = i, per, self.n

            def leave(self, trips):
                assert self.n - self.mark == self.per, (self.n - self.mark, self.per)
                self.n = self.mark + trips * self.per
                self.i = None

        ROPES = [("kr", R_MISC)] + [(64, tile) for tile in (A_Q, A_Q + 1, A_K, D_Q, D_Q + 1, D_K)] + [("q", h) for h in range(4)]

        HEADS = [(h, h // 2, slice(64 * (h % 2), 64 * (h % 2) + 64)) for h in range(4)]

        def own_half(o, half):
            return ps[:, o:o + 512].rearrange("p (f c) -> p f c", f=2)[:, :, half * 192:half * 192 + 64]

        block = ctx.enter_context(nc.Block())

        @block.sync
        def _(sp):
            sp.dma_start(cT[:, :], cT_d).then_inc(s_const, 16)
            sp.dma_start(pcol[:, :].rearrange("p (l n) -> p l n", l=DEPTH),
                         pcol_d.rearrange("l p n -> p l n")).then_inc(s_const, 16)
            sp.dma_start(kf[:, :], constf_d).then_inc(s_const, 16)
            used = [0]

            def stream(src, first, n):
                with sp.Fori(0, n // SLOTS) as i:
                    for q in range(SLOTS):
                        sp.wait_ge(s_tile[q], 1 + used[0] + i)
                        sp.dma_start(slab[:, q * SLAB:(q + 1) * SLAB],
                                     src[ds(first + i * SLOTS + q, 1), :, :].rearrange("a p n -> (a p) n")
                                     ).then_inc(s_slab[q], 16)
                used[0] += n // SLOTS

            for l in range(DEPTH):
                stream(wmod_d, l * NMOD, NMOD)
                if l == 0:
                    for k in range(KT):
                        sp.dma_start(xv[:, k, :], xT_d[:, k, :]).then_inc(s_x, 16)
                    sp.dma_start(zT[:, 0:NKM * P], constm_d).then_inc(s_maskraw, 16)
                stream(win_d, l * NZ, NZ)
                stream(wout_d, l * KT, KT)
                with sp.Fori(0, FFG) as i:
                    for half, src in ((0, w1_d), (1, w2_d)):
                        for k in range(KT):
                            q = k % SLOTS
                            sp.wait_ge(s_tile[q], 1 + i * 4 + (used[0] + 2 * half + k // SLOTS))
                            sp.dma_start(slab[:, q * SLAB:(q + 1) * SLAB],
                                         src[ds(i * KT + (l * FFG * KT + k), 1), :, :].rearrange("a p n -> (a p) n")
                                         ).then_inc(s_slab[q], 16)
                used[0] += 4 * FFG
            sp.wait_ge(s_xup, DEPTH * 2 * KT)
            sp.dma_start(out_d, xv[:, :, 0:LAT]).then_inc(s_out, 16)
            sp.wait_ge(s_out, 16)

        @block.gpsimd
        def _(pool):
            ch = Chain(pool, s_pool)
            for first in (s_S, s_ev, s_ev2, s_modrow, s_P, s_pta, s_ptd, s_on, *s_tile, *s_y, *s_kv, *s_Sn, *s_AR, *s_BK,
                          *s_ye, *s_Us):
                pool.sem_inc(first, 1)
            for l in range(DEPTH):
                pool.wait_ge(s_modT, l + 1)
                for dst, src in ((rope, rope_d), (wmask, wmask_d), (uq, uq_d[l]), (ukv, ukv_d[l])):
                    pool.dma_start(dst, src).then_inc(s_atab, 16)
                pool.memset(vD[:, 0, :], 0.0)
                pool.memset(vD[:, 5, :], 0.0).then_inc(s_pads, 1)
                pool.wait_ge(s_pair, 12 * l + 2)
                pool.memset(zv[:, D_V, 0:P], 0.0)
                pool.memset(zv[:, D_V, P + LAT:TOK], 0.0).then_inc(s_pads, 1)
                pool.wait_ge(s_pair, 12 * (l + 1))
                pool.wait_ge(s_roped, 11 * l + 7)
                pool.wait_ge(s_pads, 2 * (l + 1))
                with pool.Fori(0, NBL) as i:
                    pool.wait_ge(s_S, 1 + (l * NB + i) * 12)
                    pool.tensor_copy(kwin, zv[:, D_V, ds(i * P, 384)]).then_inc(s_kw, 1)

                pool.wait_ge(s_on, 1 + 12 * (l * NB + (NB if l == 0 else NBL)))
                for i, (dst, src) in enumerate(((w2a2, w2a2_d[l]), (g2a, g2_d[l, :, 0:256]), (g2b, g2_d[l, 0:32, 256:512]),
                                                (smask, smask_d))):
                    pool.dma_start(dst, src).then_inc(s_rtab, 16)
                zr = zv[:, R_R:NZ, :]
                for k in range(9):
                    pool.tensor_tensor(uS[:, k, 1:TOK - 1], zr[:, k, 0:TOK - 2], zr[:, k, 2:TOK], ALU.add)
                    ch.link(pool.tensor_copy(uS[:, k, 0:1], zr[:, k, 1:2]))
                    pool.tensor_copy(uS[:, k, LAT - 1:LAT], zr[:, k, LAT - 2:LAT - 1])
                    pool.tensor_copy(uS[:, k, LAT:LAT + 1], zr[:, k, LAT + 1:LAT + 2])
                    pool.tensor_copy(uS[:, k, TOK - 1:TOK], zr[:, k, TOK - 2:TOK - 1]).then_inc(s_ush, 1)
                pool.wait_ge(s_shift, 9 * (l + 1))
                pool.dma_start(lnw, ln_d[l, :, 0:256]).then_inc(s_ln, 16)
                pool.dma_start(lnb, ln_d[l, :, 256:512]).then_inc(s_ln, 16)
                pool.wait_ge(s_prep, 5 * l + 4)
                for f in range(2):
                    ch.link(pool.tensor_tensor(bonus_in[:, f, :], kd[:, f, :], kd[:, 2 + f, :], ALU.add))
                    pool.tensor_tensor(bonus_in[:, f, :], bonus_in[:, f, :], zv[:, R_R + f, :],
                                       ALU.mult).then_inc(s_bonin, 1)

                pool.wait_ge(s_prep, 5 * l + 5)
                step0 = NB * l
                for n, b0 in SCAN:
                    with pool.Fori(0, n) as i:
                        ch.enter(i, 2)
                        for g in range(2):
                            r = G[g]
                            off = i * P + b0 * P if g == 0 else i * (-P) + (b0 + n - 1) * P
                            vof = i * 256 + b0 * 256 if g == 0 else i * (-256) + (b0 + n - 1) * 256
                            pool.wait_ge(s_E[g], i + (step0 + 1))
                            pool.wait_ge(s_y[g], 1 + i + step0)
                            pool.tensor_tensor(r["bt"], bh[:, 2 * g:2 * g + 2, ds(off, P)], r["ei"], ALU.mult)
                            pool.tensor_tensor(r["kt"], kd[:, 2 * g:2 * g + 2, ds(off, P)], r["ei"],
                                               ALU.mult).then_inc(s_BK[g], 1)
                            pool.tensor_copy(r["vs"], zT[:, ds(vof + 8 * TOK, 256)]).then_inc(s_V[g], 1)
                        for g in range(2):
                            r = G[g]
                            pool.wait_ge(s_msk[g], (i + step0) * 3 + 1)
                            pool.wait_ge(s_kv[g], 1 + (i + step0) * 2)
                            ch.link(pool.tensor_tensor(
                                r["tt"], r["abr"][:, :, 0:P],
                                mask(g, 3).unsqueeze(1).to_broadcast([P, 4, P]), ALU.mult))
                            pool.tensor_tensor(r["tt"], r["tt"], ident.unsqueeze(1).to_broadcast([P, 4, P]),
                                               ALU.add).then_inc(s_tti[g], 1)
                        ch.leave(n)
                    step0 = step0 + n

        @block.scalar
        def _(act):
            nc_ = nc.scalar

            def par(l, name, k=0):
                return pcol[:, l * NPC + PC[name] + k:l * NPC + PC[name] + k + 1]

            act.wait_ge(s_const, 48)
            nc_.activation(silu[:, :], cT[:, :], ACT.Sigmoid).then_inc(s_silu, 1)

            def squares(l, which, src):
                t = TOK if which == 0 or l < DEPTH - 1 else LAT
                if which == 1:
                    act.wait_ge(s_ev, 1 + 60 * l + 28)
                if which == 3:
                    act.wait_ge(s_ev2, 1 + 32 * (l + 1))
                if which == 2:
                    act.wait_ge(s_xup, 8 * (2 * l + 1))
                if which == 0 and l:
                    act.wait_ge(s_xup, 16 * l)
                for k in range(KT):
                    nc_.activation(sq[:, k, 0:t], src[:, k, 0:t], ACT.Square).then_inc(s_sq, 1)

            def root(n, t):
                act.wait_ge(s_ms, n + 1)
                nc_.activation(rs[:, 0:t], rs[:, 0:t], ACT.Sqrt).then_inc(s_rt, 1)

            def shifted(l, which):
                for k in range(KT):
                    act.wait_ge(s_xn, 16 * l + (8 if which == 2 else 0) + k + 1)
                    for s, a, b in segs(l, which == 2):
                        ins = nc_.activation(hv[:, k, a:b], hv[:, k, a:b], ACT.Identity,
                                             scale=gv[:, which, k, s:s + 1],
                                             bias=mv[:, (24 if which == 2 else 0) + k, s:s + 1])
                    ins.then_inc(s_h, 1)

            for l in range(DEPTH):
                with act.Fori(0, 12) as i:
                    act.wait_ge(s_tile[3], 1 + i + (FILLS * l + 1))
                    nc_.activation(work[0:2, ds(i * 512, 512)], ps[0:2, 3584:4096], ACT.Copy).then_inc(s_modrow, 1)
                if l == 0:
                    act.wait_ge(s_x, 16 * KT)
                squares(l, 0, xv)
                root(4 * l, TOK)
                shifted(l, 0)
                act.wait_ge(s_masks, 1)
                with act.Fori(0, NZ // SLOTS) as i:
                    for q in range(SLOTS):
                        act.wait_ge(s_tile[q], 1 + i + (FILLS * l + F_IN + 1))
                        nc_.activation(zT[:, ds(i * (SLOTS * TOK) + q * TOK, TOK)],
                                       ps[:, (q % 2) * 1024:(q % 2) * 1024 + TOK], ACT.Copy).then_inc(s_ev, 1)
                act.wait_ge(s_ev, 1 + 60 * l + NZ)
                for n, tile in enumerate((A_Q, A_Q + 1, A_K, C_Q, C_Q + 1, C_KV)):
                    nc_.activation(work[:, n * TOK:(n + 1) * TOK], zv[:, tile, :], ACT.Square).then_inc(s_psq, 1)
                for n, (width, bank) in enumerate(((64, 0), (64, 2), (64, 4), (256, 6), (128, 0))):
                    act.wait_ge(s_pss, 5 * l + n + 1)
                    nc_.activation(work[:, W_P + n * TOK:W_P + (n + 1) * TOK], ps[:, bank * 512:bank * 512 + TOK],
                                   ACT.Sqrt, scale=1.0 / width, bias=eps[:, 0:1]).then_inc(s_prt, 1)
                for n in range(12):
                    act.wait_ge(s_pair, 12 * l + n + 1)
                    o = (n % 2) * 3072
                    if n == 0:
                        ins = nc_.activation(wv(W_VA, TOK), ps[:, o:o + TOK], ACT.Copy)
                    elif n == 1:
                        nc_.activation(wv(W_VD + P, LAT), ps[:, o:o + LAT], ACT.Copy)
                        ins = nc_.activation(wv(W_VD + 6 * P, CTX), ps[:, o + LAT:o + TOK], ACT.Copy)
                    elif n < 6:
                        ins = nc_.activation(qB[0:96, n - 2, :], ps[0:96, o:o + TOK], ACT.Copy)
                    elif n < 10:
                        ins = nc_.activation(kB[0:64, n - 6, :], ps[0:64, o:o + TOK], ACT.Copy)
                    elif n == 10:
                        ins = nc_.activation(wv(W_VB, 1024), ps[:, o:o + 1024], ACT.Copy)
                    else:
                        ins = nc_.activation(wv(W_VB + 1024, 512), ps[:, o:o + 512], ACT.Copy)
                    ins.then_inc(s_paire, 1)
                act.wait_ge(s_roped, 11 * l + 1)
                nc_.activation(kB[64:96], zv[64:96, R_MISC, :].unsqueeze(1).to_broadcast([32, 4, TOK]),
                               ACT.Copy).then_inc(s_krc, 1)
                act.wait_ge(s_roped, 11 * (l + 1))
                for n, b0 in streams(l):
                    nk = NB if b0 == 0 else NBC
                    with act.Fori(0, n) as i:
                        it = i + (l * NB + b0)
                        off = i * P + b0 * P
                        act.wait_ge(s_S, 1 + it * 12)
                        for g in range(2):
                            rows = slice(64 * g, 64 * g + 64)
                            for q, tile in ((qa, A_Q), (qd, D_Q)):
                                nc_.activation(q[rows, 2 * g:2 * g + 2, :], zv[rows, tile:tile + 2, ds(off, P)],
                                               ACT.Copy, scale=0.125)
                        nc_.activation(qb[0:96], qB[0:96, :, ds(off, P)], ACT.Copy, scale=96.0 ** -0.5).then_inc(s_qt, 1)

                        def exps(h):
                            act.wait_ge(s_nm, it * 12 + (h + 1))
                            masked = h >= 8 and b0 == 0
                            w = 640 if masked else nk * P
                            if h >= 2:
                                act.wait_ge(s_T, it * 12 + (h - 1))
                            src = prob[:, h % 2, 0:w] if masked else ps[:, (h % 2) * 1024:(h % 2) * 1024 + w]
                            nc_.activation(prob[:, h % 2, 0:w], src, ACT.Exp, bias=small[:, h:h + 1],
                                           accum_out=small[:, 16 + h:17 + h]).then_inc(s_P, 1)
                            if h >= 8:
                                nc_.activation(small[:, 32 + h:33 + h], par(l, "sink", h - 8), ACT.Exp,
                                               bias=small[:, h:h + 1]).then_inc(s_es, 1)

                        def turned(h):
                            act.wait_ge(s_T, it * 12 + (h + 1))
                            if h >= 2:
                                act.wait_ge(s_O, it * 12 + (h - 1))
                            w = LAT if nk == NB else P
                            nc_.activation(probT[:, h % 2, 0:w], ps[:, 2048:2048 + w], ACT.Copy).then_inc(s_pta, 1)

                        exps(0)
                        exps(1)
                        for h in range(12):
                            turned(h)
                            if h < 10:
                                exps(h + 2)
                for k in range(9):
                    act.wait_ge(s_ush, 9 * l + k + 1)
                    nc_.activation(zv[:, R_R + k, :], zv[:, R_R + k, :], ACT.Identity,
                                   scale=omm[:, k:k + 1]).then_inc(s_zs, 1)
                act.wait_ge(s_shift, 9 * (l + 1))
                nc_.activation(zv[0:64, R_WA, :], zv[0:64, R_WA, :], ACT.Tanh)
                nc_.activation(zv[:, R_GL, :], zv[:, R_GL, :], ACT.Sigmoid)
                nc_.activation(zv[0:32, R_MISC, :], zv[0:32, R_MISC, :], ACT.Sigmoid).then_inc(s_gate, 1)
                for n in range(12):
                    act.wait_ge(s_rp, 12 * l + n + 1)
                    o = (n % 2) * 1024
                    if n < 2:
                        ins = nc_.activation(vtok[:, :, n * P:(n + 1) * P],
                                             ps[:, o:o + TOK].rearrange("p (b f) -> p b f", b=NB), ACT.Copy)
                    elif n == 2:
                        ins = nc_.activation(gtok[:, 0:4, :], ps[:, o:o + 1024].rearrange("p (b f) -> p b f", b=4), ACT.Copy)
                    elif n == 3:
                        ins = nc_.activation(gtok[:, 4:6, :], ps[:, o:o + 512].rearrange("p (b f) -> p b f", b=2), ACT.Copy)
                    elif n < 8:
                        ins = nc_.activation(sg[:, n - 4, :], ps[:, o:o + TOK], ACT.Sigmoid, bias=par(l, "w0", n - 4))
                    else:
                        ins = nc_.activation(aa[:, n - 8, :], ps[:, o:o + TOK], ACT.Sigmoid, bias=par(l, "a0", n - 8))
                    ins.then_inc(s_rpe, 1)
                for n in range(4):
                    act.wait_ge(s_kk, 4 * l + n + 1)
                    nc_.activation(rn[:, n, :], nkk[:, n, :], ACT.Square).then_inc(s_kkq, 1)
                for n in range(4):
                    act.wait_ge(s_kks, 4 * l + n + 1)
                    o = 2048 + (n % 2) * 1024
                    nc_.activation(rn[:, n, :], ps[:, o:o + TOK], ACT.Sqrt).then_inc(s_kkr, 1)
                act.wait_ge(s_bonin, 2 * (l + 1))
                for f in range(2):
                    ins = nc_.activation(bonus_in[:, f, :], bonus_in[:, f, :], ACT.Identity, scale=par(l, "r_k", f))
                ins.then_inc(s_gate, 1)
                act.wait_ge(s_bonps, l + 1)
                nc_.activation(bon[:, :], ps[:, 3584:3584 + NB * 4], ACT.Copy).then_inc(s_bon, 1)
                act.wait_ge(s_prep, 5 * l + 5)
                step0 = NB * l
                for n, b0 in SCAN:
                    with act.Fori(0, n) as i:
                        it = i + step0
                        for g in range(2):
                            r = G[g]
                            off = i * P + b0 * P if g == 0 else i * (-P) + (b0 + n - 1) * P
                            act.wait_ge(s_Sn[g], 1 + it * 2)
                            act.wait_ge(s_AR[g], 1 + it)
                            act.wait_ge(s_BK[g], 1 + it)
                            lo = 1 if g == 0 else 0
                            for f in range(2):
                                nc_.activation(r["ep"][:, f, :, lo:lo + 64],
                                               cs[:, 2 * g + f, ds(off, P)].rearrange("p (c t) -> p c t", c=2),
                                               ACT.Exp, scale=-DECAY)
                            nc_.activation(r["ei"], cs[:, 2 * g:2 * g + 2, ds(off, P)], ACT.Exp,
                                           scale=DECAY).then_inc(s_E[g], 1)
                        for g in range(2):
                            r = G[g]
                            act.wait_ge(s_pre[g], it * 4 + 3)
                            nc_.activation(r["tok"], ps[:, g * 2048:g * 2048 + 1024], ACT.Copy).then_inc(s_tok[g], 1)
                        for g in range(2):
                            r = G[g]
                            act.wait_ge(s_kv[g], 1 + it * 2 + 1)
                            o = g * 2048 + 1536
                            for half in range(2):
                                ins = nc_.activation(r["akv"][:, half::2, :], own_half(o, half), ACT.Copy)
                            ins.then_inc(s_kve[g], 1)
                        for g in range(2):
                            r = G[g]
                            act.wait_ge(s_W[g], it + 1)
                            nc_.activation(r["wt"], ps[:, g * 2048 + 1024:g * 2048 + 1536].rearrange("p (h t) -> p h t", h=4),
                                           ACT.Copy).then_inc(s_Wt[g], 1)
                            act.wait_ge(s_kv[g], 1 + it * 2 + 2)
                            o = g * 2048
                            for half in range(2):
                                ins = nc_.activation(r["uv"][:, half::2, :], own_half(o, half), ACT.Copy)
                            ins.then_inc(s_kve[g], 1)
                        for g in range(2):
                            act.wait_ge(s_y[g], 1 + it + 1)
                            bof = i + b0 if g == 0 else i * (-1) + (b0 + n - 1)
                            for c in range(2):
                                slot = c if g == 0 else 1 - c
                                if g == 0:
                                    dst = hT[64 * c:64 * c + 64, ds(bof * 1024 + 512, 256)]
                                else:
                                    dst = zT[64 * c:64 * c + 64, ds(bof * 256 + R_K * TOK, 256)]
                                src = ps[64 * c:64 * c + 64, g * 2048 + 1024:g * 2048 + 1536].rearrange(
                                    "p (h s i) -> p h s i", h=4, s=2)[:, :, slot, :]
                                ins = nc_.activation(dst.rearrange("p (h i) -> p h i", h=4), src, ACT.Copy)
                            ins.then_inc(s_ye[g], 1)
                    step0 = step0 + n
                nbk = NB if l < DEPTH - 1 else NBL
                act.wait_ge(s_rout, 2 * l + 1)
                nc_.activation(small[:, 48:48 + 4 * nbk], small[:, 48:48 + 4 * nbk], ACT.Sqrt).then_inc(s_rt, 1)
                for f in range(KT):
                    act.wait_ge(s_ot, KT * l + f + 1)
                    t = nbk * P
                    nc_.activation(oT[:, f, 0:t], ps[:, (f % 2) * 1024:(f % 2) * 1024 + t], ACT.Copy).then_inc(s_ote, 1)
                t = TOK if l < DEPTH - 1 else LAT
                with act.Fori(0, KT // SLOTS) as i:
                    for q in range(SLOTS):
                        act.wait_ge(s_tile[q], 1 + i + (FILLS * l + F_OUT + 1))
                        nc_.activation(zT[:, ds(i * (SLOTS * TOK) + q * TOK, t)],
                                       ps[:, (q % 2) * 1024:(q % 2) * 1024 + t], ACT.Copy).then_inc(s_ev, 1)
                squares(l, 1, yT)
                root(4 * l + 1, t)
                squares(l, 2, xv)
                root(4 * l + 2, t)
                shifted(l, 2)
                with act.Fori(0, FFG) as i:
                    act.wait_ge(s_tile[3], 1 + i * 4 + (FILLS * l + F_MLP))
                    for k in range(KT):
                        act.wait_ge(s_tile[k % SLOTS], 1 + i * 4 + (FILLS * l + F_MLP + k // SLOTS + 1))
                        nc_.activation(h1[:, k, 0:t], ps[:, (k % 2) * 1024:(k % 2) * 1024 + t],
                                       ACT.Relu).then_inc(s_ev, 1)
                squares(l, 3, yT)
                root(4 * l + 3, t)

        @block.vector
        def _(dve):
            ch = Chain(dve, s_dve)
            V = nc.vector

            def pars(l, name, n, k=0):
                return pcol[:, l * NPC + PC[name] + k:l * NPC + PC[name] + k + n]

            V.memset(eps[:, :], EPS).then_inc(s_gain, 1)
            dve.wait_ge(s_silu, 1)
            V.tensor_tensor(silu[:, :], silu[:, :], cT[:, :], ALU.mult).then_inc(s_silu, 1)
            dve.wait_ge(s_maskraw, 16)
            V.tensor_copy(km[:, :], zT[:, 0:NKM * P]).then_inc(s_masks, 1)

            def mean_root(n, t):
                dve.wait_ge(s_ssq, n + 1)
                V.tensor_scalar(rs[:, 0:t], ps[:, 3072:3072 + t], 1.0 / DM, EPS, ALU.mult, ALU.add).then_inc(s_ms, 1)
                dve.wait_ge(s_rt, n + 1 + gn_roots(n))
                ch.link(V.reciprocal(rs[:, 0:t], rs[:, 0:t]))

            def gn_roots(n):
                return n // 4 + (1 if n % 4 else 0)

            def pre(l, which):
                t = TOK if which == 0 or l < DEPTH - 1 else LAT
                mean_root(4 * l + which, t)
                for k in range(KT):
                    V.tensor_tensor(hv[:, k, 0:t], xv[:, k, 0:t], rs[:, 0:t], ALU.mult).then_inc(s_xn, 1)

            def post(l, which):
                t = TOK if l < DEPTH - 1 else LAT
                mean_root(4 * l + which, t)
                for k in range(KT):
                    ch.link(V.tensor_tensor(yT[:, k, 0:t], yT[:, k, 0:t], rs[:, 0:t], ALU.mult))
                    for s, a, b in segs(l, True):
                        ins = V.scalar_tensor_tensor(out=xv[:, k, a:b], in0=yT[:, k, a:b], scalar=gv[:, which, k, s:s + 1],
                                                     in1=xv[:, k, a:b], op0=ALU.mult, op1=ALU.add)
                    ins.then_inc(s_xup, 1)

            for l in range(DEPTH):
                dve.wait_ge(s_modps, l + 1)
                if l:
                    dve.wait_ge(s_h, 16)
                ch.link(V.tensor_tensor(mv, ps[:, 3584:3584 + 2 * NMOD].rearrange("p (k s) -> p k s", s=2),
                                        pars(l, "b_mod", NMOD).unsqueeze(2).to_broadcast([P, NMOD, 2]), ALU.add))
                for n, (name, part, plus) in enumerate((("g_pre_mix", 8, 1), ("g_post_mix", 16, 0),
                                                        ("g_pre_mlp", 32, 1), ("g_post_mlp", 40, 0))):
                    if plus:
                        ch.link(V.tensor_scalar(gv[:, n], mv[:, part:part + 8, :], 1.0, None, ALU.add))
                    V.tensor_tensor(gv[:, n], gv[:, n] if plus else mv[:, part:part + 8, :],
                                    pars(l, name, 8).unsqueeze(2).to_broadcast([P, 8, 2]), ALU.mult)
                V.tensor_scalar(omm[:, 0:9], pars(l, "mu", 9), -1.0, 1.0, ALU.mult, ALU.add)
                V.tensor_scalar(omm[:, 9:18], pars(l, "mu", 9), 0.5, None, ALU.mult)
                V.tensor_scalar(omm[:, 18:22], pars(l, "k_a", 4), -1.0, 1.0, ALU.mult, ALU.add)
                ch.link(V.tensor_scalar(omm[:, 22:26], pars(l, "sink", 4), -1.0, None, ALU.mult))
                dve.sem_inc(s_modT, 1)
                pre(l, 0)

                for n, (tile, name) in enumerate(((A_Q, "q_norm"), (A_Q + 1, "q_norm"), (A_K, "k_norm"),
                                                  (C_Q, "cq_norm"), (C_KV, "ckv_norm"))):
                    dve.wait_ge(s_prt, 5 * l + n + 1)
                    r = work[:, W_P + n * TOK:W_P + (n + 1) * TOK]
                    ch.link(V.reciprocal(r, r))
                    for j in range(2 if tile == C_Q else 1):
                        V.scalar_tensor_tensor(out=zv[:, tile + j, :], in0=zv[:, tile + j, :], scalar=pars(l, name, 1, j),
                                               in1=r, op0=ALU.mult, op1=ALU.mult).then_inc(s_pn, 1)
                dve.wait_ge(s_atab, 64 * (l + 1))
                for n, (where, tile) in enumerate(ROPES):
                    p = 96 if where != 64 else P
                    tab = 2 if where != 64 else 0
                    x = qB[0:p, tile, 0:LAT] if where == "q" else zv[0:p, tile, 0:LAT]
                    dst = zv[:, D_V, P:P + LAT] if tile == D_K and where == 64 else x
                    o = 1024 + (n % 4) * 512
                    tmp = work[0:p, W_PT + (n % 2) * LAT:W_PT + (n % 2) * LAT + LAT]
                    dve.wait_ge(s_rot, 11 * l + n + 1)
                    V.tensor_tensor(tmp, ps[0:p, o:o + LAT], rope[0:p, tab + 1, :], ALU.mult)
                    ch.link(V.tensor_tensor(x, x, rope[0:p, tab, :], ALU.mult))
                    if tile == D_K and where == 64:
                        dve.wait_ge(s_pair, 12 * l + 2)
                    V.tensor_tensor(dst, x, tmp, ALU.add).then_inc(s_roped, 1)

                dve.wait_ge(s_paire, 12 * (l + 1))
                for q in (qa, qd):
                    for g in range(2):
                        ins = V.memset(q[64 - 64 * g:128 - 64 * g, 2 * g:2 * g + 2, :], 0.0)
                ins.then_inc(s_qz, 1)
                for n, b0 in streams(l):
                    nk = NB if b0 == 0 else NBC
                    win = b0 == 0
                    with dve.Fori(0, n) as i:
                        it = i + (l * NB + b0)
                        ch.enter(i, (8 if win else 4) + 12 + 4)

                        def peak(h):
                            dve.wait_ge(s_S, 1 + it * 12 + (h + 1))
                            o = (h % 2) * 1024
                            src = ps[:, o:o + nk * P]
                            if h >= 8 and win:
                                dve.wait_ge(s_T, it * 12 + (h - 1))
                                V.tensor_tensor(prob[:, h % 2, 0:384], ps[:, o:o + 384],
                                                work[:, ds(i * 384 + W_WMASK, 384)], ALU.add)
                                ch.link(V.tensor_copy(prob[:, h % 2, 384:640], ps[:, o + 512:o + TOK]))
                                src = prob[:, h % 2, 0:640]
                            nm = small[:, h:h + 1]
                            ins = V.tensor_reduce(nm, src, AX.X, ALU.max, negate=True)
                            if h >= 8:
                                ch.link(ins)
                                V.tensor_tensor(nm, nm, omm[:, 22 + h - 8:23 + h - 8], ALU.min).then_inc(s_nm, 1)
                            else:
                                ins.then_inc(s_nm, 1)

                        def turned(h):
                            dve.wait_ge(s_T, it * 12 + (h + 1))
                            if h >= 2:
                                dve.wait_ge(s_O, it * 12 + (h - 1))
                            a = LAT if win else P
                            n_ = P if h >= 8 or not win else CTX
                            V.tensor_copy(probT[:, h % 2, a:a + n_], ps[:, 2560:2560 + n_]).then_inc(s_ptd, 1)

                        def normed(h):
                            sm = small[:, 16 + h:17 + h]
                            dve.wait_ge(s_P, 1 + it * 12 + (h + 1))
                            if h >= 8:
                                dve.wait_ge(s_es, it * 4 + (h - 7))
                                ch.link(V.tensor_tensor(sm, sm, small[:, 32 + h:33 + h], ALU.add))
                            ch.link(V.reciprocal(sm, sm))
                            dve.wait_ge(s_O, it * 12 + (h + 1))
                            grp, hh = h // 4, h % 4
                            col = (0, 256, 768)[grp] + hh * 64
                            half = (hh % 2) if grp == 1 else hh // 2
                            o = 3072 + (h % 2) * 512 + half * 64
                            V.tensor_scalar(hT[:, ds(i * 1024 + (b0 * 1024 + col), 64)], ps[:, o:o + 64], sm, None,
                                            ALU.mult).then_inc(s_on, 1)

                        peak(0)
                        peak(1)
                        for h in range(12):
                            turned(h)
                            if h < 10:
                                peak(h + 2)
                            normed(h)
                        ch.leave(n)

                for k in range(9):
                    dve.wait_ge(s_zs, 9 * l + k + 1)
                    V.scalar_tensor_tensor(out=zv[:, R_R + k, :], in0=uS[:, k, :], scalar=omm[:, 9 + k:10 + k],
                                           in1=zv[:, R_R + k, :], op0=ALU.mult, op1=ALU.add).then_inc(s_shift, 1)
                dve.wait_ge(s_shift, 9 * (l + 1))
                for n in range(4):
                    V.tensor_scalar(nkk[:, n, :], zv[:, R_K + n % 2, :], pars(l, "k_k", 1, n), None,
                                    ALU.mult).then_inc(s_kk, 1)
                dve.wait_ge(s_rtab, 64 * (l + 1))
                for n in range(4):
                    dve.wait_ge(s_rpe, 12 * l + 8 if n == 0 else 12 * l + 8)
                    if n == 0:
                        dve.wait_ge(s_rp, 12 * (l + 1))
                    ch.link(V.tensor_tensor_scan(cs[:, n, :], smask, sg[:, n, :], 0.0, ALU.mult, ALU.add))
                    if n >= 2:
                        ch.link(V.tensor_tensor(sg[:, n, :], sg[:, n, :], cs[:, n, :], ALU.subtract))
                        c3 = cs[:, n, :].rearrange("p (c t) -> p c t", t=CH)
                        s3 = sg[:, n, :].rearrange("p (c t) -> p c t", t=CH)
                        ch.link(V.tensor_tensor(s3, s3, c3[:, :, CH - 1:CH].to_broadcast([P, TOK // CH, CH]), ALU.add))
                        ch.link(V.tensor_copy(cs[:, n, :], sg[:, n, :]))
                dve.wait_ge(s_rpe, 12 * (l + 1))
                for n in range(4):
                    dve.wait_ge(s_kkr, 4 * l + n + 1)
                    ch.link(V.tensor_scalar(rn[:, n, :], rn[:, n, :], 1e-12, None, ALU.max))
                    ch.link(V.reciprocal(rn[:, n, :], rn[:, n, :]))
                    ch.link(V.scalar_tensor_tensor(out=nkk[:, n, :], in0=nkk[:, n, :], scalar=-1.0, in1=rn[:, n, :],
                                                   op0=ALU.mult, op1=ALU.mult))
                    ch.link(V.scalar_tensor_tensor(out=bh[:, n, :], in0=nkk[:, n, :], scalar=-1.0, in1=aa[:, n, :],
                                                   op0=ALU.mult, op1=ALU.mult))
                for n in range(4):
                    ch.link(V.tensor_scalar(aa[:, n, :], aa[:, n, :], pars(l, "k_a", 1, n), omm[:, 18 + n:19 + n],
                                            ALU.mult, ALU.add))
                    V.tensor_tensor(kd[:, n, :], aa[:, n, :], zv[:, R_K + n % 2, :], ALU.mult).then_inc(s_prep, 1)
                for g in range(2):
                    lo = 0 if g == 0 else 64
                    V.memset(G[g]["ep"][:, :, :, lo:lo + 1], 1.0)
                    for h, f, rows in HEADS:
                        V.memset(G[g]["ar"][64 - rows.start:128 - rows.start, h, :, :], 0.0)
                    ch.link(V.memset(st[g], 0.0))
                dve.sem_inc(s_prep, 1)

                step0 = NB * l
                for n, b0 in SCAN:
                    with dve.Fori(0, n) as i:
                        it = i + step0
                        ch.enter(i, 2 * (1 + 2))
                        for g in range(2):
                            r = G[g]
                            off = i * P + b0 * P if g == 0 else i * (-P) + (b0 + n - 1) * P
                            lo = (0, 1) if g == 0 else (1, 0)
                            dve.wait_ge(s_E[g], it + 1)
                            dve.wait_ge(s_y[g], 1 + it)
                            for h, f, rows in HEADS:
                                for j, src in enumerate((nkk[rows, 2 * g + f, ds(off, P)], zv[rows, R_R + f, ds(off, P)])):
                                    ins = V.tensor_tensor(r["ar"][rows, h, j, :].rearrange("p (c t) -> p c t", c=2),
                                                          src.rearrange("p (c t) -> p c t", c=2),
                                                          r["ep"][rows, f, :, lo[j]:lo[j] + 64], ALU.mult)
                            ins.then_inc(s_AR[g], 1)
                        for g in range(2):
                            r = G[g]
                            m2 = mask(g, 0, 2).unsqueeze(1).to_broadcast([P, 4, 256])
                            dve.wait_ge(s_pre[g], it * 4 + 1)
                            V.tensor_tensor(r["abr"], ps[:, g * 2048:g * 2048 + 1024].rearrange("p (h t) -> p h t", h=4),
                                            m2, ALU.mult).then_inc(s_msk[g], 1)
                            dve.wait_ge(s_pre[g], it * 4 + 2)
                            V.tensor_tensor(r["akr"], ps[:, g * 2048 + 1024:g * 2048 + 2048].rearrange(
                                "p (h t) -> p h t", h=4), m2, ALU.mult).then_inc(s_msk[g], 1)
                        for g in range(2):
                            r = G[g]
                            dve.wait_ge(s_pre[g], it * 4 + 4)
                            ch.link(V.tensor_tensor(r["t"], ps[:, g * 2048 + 1024:g * 2048 + 1536].rearrange(
                                "p (h t) -> p h t", h=4), mask(g, 2).unsqueeze(1).to_broadcast([P, 4, P]), ALU.mult))
                            V.tensor_tensor(r["t"], r["t"], ident.unsqueeze(1).to_broadcast([P, 4, P]),
                                            ALU.add).then_inc(s_msk[g], 1)
                        for j in range(len(LEVELS)):
                            for g in range(2):
                                dve.wait_ge(s_X[g], it * 5 + (j + 1))
                                V.tensor_tensor(G[g]["x"], ps[:, g * 2048 + 1536:g * 2048 + 2048].rearrange(
                                    "p (h t) -> p h t", h=4), mask(g, 4 + j).unsqueeze(1).to_broadcast([P, 4, P]),
                                    ALU.mult).then_inc(s_Xm[g], 1)
                            for g in range(2):
                                r = G[g]
                                if j < 4:
                                    dve.wait_ge(s_Tp[g], it * 9 + (2 * j + 2))
                                    V.tensor_tensor(r["t"], r["t"], ps[:, g * 2048:g * 2048 + 512].rearrange(
                                        "p (h t) -> p h t", h=4), ALU.add).then_inc(s_Tu[g], 1)
                                else:
                                    dve.wait_ge(s_Tp[g], it * 9 + 9)
                                V.tensor_tensor(r["tt"], r["tt"], ps[:, g * 2048 + 512:g * 2048 + 1024].rearrange(
                                    "p (h t) -> p h t", h=4), ALU.add).then_inc(s_Tu[g], 1)
                        for k in range(2):
                            for g in range(2):
                                r = G[g]
                                c = k if g == 0 else 1 - k
                                rows = slice(64 * c, 64 * c + 64)
                                dve.wait_ge(s_U[g], it * 2 + (k + 1))
                                if k == 0:
                                    dve.wait_ge(s_kve[g], it * 2 + 2)
                                V.tensor_tensor(r["u"][rows], ps[rows, g * 2048 + 512:g * 2048 + 1024].rearrange(
                                    "p (h s i) -> p h s i", h=4, s=2)[:, :, k, :], r["uv"][rows],
                                    ALU.add).then_inc(s_Us[g], 1)
                            for g in range(2):
                                r = G[g]
                                c = k if g == 0 else 1 - k
                                end = 64 if g == 0 else 0
                                dve.wait_ge(s_dS[g], it * 2 + (k + 1))
                                ch.link(V.tensor_tensor(s1[g], st[g][:, :, k, :], ps[:, g * 2048 + 1536:g * 2048 + 1664]
                                                        .rearrange("p (f i) -> p f i", f=2), ALU.add))
                                if k == 1:
                                    dve.wait_ge(s_y[g], 1 + it + 1)
                                V.tensor_tensor(st[g][:, :, 1 - k, :], s1[g],
                                                r["ep"][:, :, c, end:end + 1].to_broadcast([P, 2, 64]),
                                                ALU.mult).then_inc(s_Sn[g], 1)
                        ch.leave(n)
                    step0 = step0 + n

                nbk = NB if l < DEPTH - 1 else NBL
                for g in range(2):
                    dve.wait_ge(s_ye[g], 1 + NB * (l + 1))
                y = yrev[:, 0:nbk, :]
                y4 = yrev[:, 0:nbk, :].rearrange("p b (h i) -> p b h i", h=4)
                vt = vtok[:, 0:nbk, :]
                v4 = vt.rearrange("p b (h i) -> p b h i", h=4)
                tmp = wv(W_SCR, NB, 256)[:, 0:nbk, :]
                t4 = tmp.rearrange("p b (h i) -> p b h i", h=4)
                mean = small[:, 72:72 + 4 * nbk]
                var = small[:, 48:48 + 4 * nbk]
                b4 = [P, nbk, 4, 64]
                ch.link(V.tensor_tensor(y, y, mix[:, 0:nbk, 512:768], ALU.add))
                ch.link(V.tensor_reduce(mean, y4, AX.X, ALU.add))
                ch.link(V.tensor_scalar(mean, mean, 1.0 / 64, None, ALU.mult))
                ch.link(V.tensor_tensor(y4, y4, mean.rearrange("p (b h) -> p b h", h=4).unsqueeze(3).to_broadcast(b4),
                                        ALU.subtract))
                ch.link(V.tensor_tensor(tmp, y, y, ALU.mult))
                ch.link(V.tensor_reduce(var, t4, AX.X, ALU.add))
                V.tensor_scalar(var, var, 1.0 / 64, GN_EPS, ALU.mult, ALU.add).then_inc(s_rout, 1)
                dve.wait_ge(s_bon, l + 1)
                ch.link(V.tensor_tensor(v4, v4, bon[:, 0:4 * nbk].rearrange("p (b h) -> p b h", h=4).unsqueeze(3)
                                        .to_broadcast(b4), ALU.mult))
                dve.wait_ge(s_rt, 5 * l + 2)
                ch.link(V.reciprocal(var, var))
                ch.link(V.tensor_tensor(y4, y4, var.rearrange("p (b h) -> p b h", h=4).unsqueeze(3).to_broadcast(b4),
                                        ALU.mult))
                dve.wait_ge(s_ln, 32 * (l + 1))
                ch.link(V.tensor_tensor(y, y, lnw.unsqueeze(1).to_broadcast([P, nbk, 256]), ALU.mult))
                ch.link(V.tensor_tensor(y, y, lnb.unsqueeze(1).to_broadcast([P, nbk, 256]), ALU.add))
                ch.link(V.tensor_tensor(y, y, vt, ALU.add))
                V.tensor_tensor(mix[:, 0:nbk, 512:768], y, gtok[:, 0:nbk, :], ALU.mult).then_inc(s_rout, 1)

                post(l, 1)
                pre(l, 2)
                t = TOK if l < DEPTH - 1 else LAT
                for k in range(KT):
                    ins = V.memset(yT[:, k, 0:t], 0.0)
                ch.link(ins)
                with dve.Fori(0, FFG) as i:
                    for k in range(KT):
                        dve.wait_ge(s_ev, 1 + i * KT + (60 * l + NZ + KT + k + 1))
                        V.tensor_tensor(h1[:, k, 0:t], h1[:, k, 0:t], h1[:, k, 0:t], ALU.mult).then_inc(s_h1, 1)
                    dve.wait_ge(s_ev2, 1 + i * KT + 32 * l)
                    for k in range(KT):
                        dve.wait_ge(s_tile[k % SLOTS], 1 + i * 4 + (FILLS * l + F_MLP + 2 + k // SLOTS + 1))
                        o = 2048 + (k % 2) * 1024
                        V.tensor_tensor(yT[:, k, 0:t], yT[:, k, 0:t], ps[:, o:o + t], ALU.add).then_inc(s_ev2, 1)
                dve.wait_ge(s_ev2, 1 + 32 * (l + 1))
                post(l, 3)

        @block.tensor
        def _(pe):
            def mm(out, lhsT, rhs, start=True, stop=True):
                return pe.matmul(out, lhsT, rhs, start=start, stop=stop)

            fills = [0]

            def product(rhs, o, q, i, t):
                pe.wait_ge(s_slab[q], i * 16 + 16 * (fills[0] + 1))
                for a, b in ((0, LAT), (LAT, TOK)) if t == TOK else ((0, LAT),):
                    for k in range(KT):
                        ins = mm(ps[:, o + a:o + b], slab[:, q * SLAB + k * P:q * SLAB + (k + 1) * P],
                                 rhs[:, k, a:b], k == 0, k == KT - 1)
                return ins

            def ssq(l, which):
                n = 4 * l + which
                t = TOK if which == 0 or l < DEPTH - 1 else LAT
                if n:
                    pe.wait_ge(s_ms, n)
                for k in range(KT):
                    pe.wait_ge(s_sq, 8 * n + k + 1)
                    for a, b in ((0, LAT), (LAT, TOK)) if t == TOK else ((0, LAT),):
                        ins = mm(ps[:, 3072 + a:3072 + b], ones, sq[:, k, a:b], k == 0, k == KT - 1)
                ins.then_inc(s_ssq, 1)

            pe.wait_ge(s_silu, 2)
            pe.wait_ge(s_const, 48)
            for l in range(DEPTH):
                t = TOK if l < DEPTH - 1 else LAT
                nbk = t // P
                if l:
                    pe.wait_ge(s_ms, 4 * l)
                with pe.Fori(0, 12) as i:
                    pe.wait_ge(s_modrow, 1 + i + 12 * l)
                    for q in range(SLOTS):
                        pe.wait_ge(s_slab[q], i * 16 + 16 * (fills[0] + 1))
                        for j in range(2):
                            k = 2 * q + j
                            ins = mm(ps[0:2, 3584:4096], silu[:, 2 * k:2 * k + 2],
                                     slab[:, q * SLAB + j * 512:q * SLAB + (j + 1) * 512], k == 0, k == KT - 1)
                        ins.then_inc(s_tile[q], 1)
                fills[0] += 12
                pe.wait_ge(s_modrow, 1 + 12 * (l + 1))
                for m in range(NMOD):
                    ins = pe.transpose(ps[:, 3584 + 2 * m:3586 + 2 * m], work[0:2, m * P:(m + 1) * P], ident[0:2, 0:2])
                ins.then_inc(s_modps, 1)
                pe.wait_ge(s_modT, l + 1)
                ssq(l, 0)
                pe.wait_ge(s_h, 16 * l + 8)
                with pe.Fori(0, NZ // SLOTS) as i:
                    for q in range(SLOTS):
                        tile = i * SLOTS + (60 * l + q)
                        if l or q >= 2:
                            pe.wait_ge(s_ev, 1 + tile - 1)
                        else:
                            pe.wait_ge(s_ev, 1 + i * SLOTS)
                        ins = product(hv, (q % 2) * 1024, q, i, TOK)
                        ins.then_inc(s_tile[q], 1)
                fills[0] += NZ // SLOTS
                for n, (first, cnt, mat, bank) in enumerate(((0, 1, bd, 0), (1, 1, bd, 2), (2, 1, bd, 4), (3, 2, ones, 6),
                                                             (5, 1, ones, 0))):
                    pe.wait_ge(s_psq, 6 * l + first + cnt)
                    if n == 0:
                        pe.wait_ge(s_ev, 1 + 60 * l + NZ)
                    if n == 4:
                        pe.wait_ge(s_prt, 5 * l + 1)
                    for a, b in ((0, LAT), (LAT, TOK)):
                        for j in range(cnt):
                            ins = mm(ps[:, bank * 512 + a:bank * 512 + b], mat,
                                     work[:, (first + j) * TOK + a:(first + j) * TOK + b], j == 0, j == cnt - 1)
                    ins.then_inc(s_pss, 1)
                pe.wait_ge(s_prt, 5 * (l + 1))

                def turn(n, tile):
                    o = (n % 2) * 3072
                    for b in range(NB):
                        ins = pe.transpose(ps[:, o + b * P:o + (b + 1) * P], zv[:, tile, b * P:(b + 1) * P], ident)
                    ins.then_inc(s_pair, 1)

                def latent(n):
                    pe.wait_ge(s_paire, 12 * l + n - 1)
                    o = (n % 2) * 3072
                    if n < 10:
                        for a, b in ((0, LAT), (LAT, TOK)):
                            if n < 6:
                                for k in range(2):
                                    ins = mm(ps[0:96, o + a:o + b], uq[:, k, (n - 2) * 96:(n - 1) * 96],
                                             zv[:, C_Q + k, a:b], k == 0, k == 1)
                            else:
                                ins = mm(ps[0:64, o + a:o + b], ukv[:, (n - 6) * P:(n - 6) * P + 64], zv[:, C_KV, a:b])
                    else:
                        vcols = ukv.rearrange("p (h c) -> p h c", h=4)[:, :, 64:128]
                        for b in (range(4) if n == 10 else range(4, 6)):
                            ins = mm(ps[:, o + (b % 4) * 256:o + (b % 4) * 256 + 256], zv[:, C_KV, b * P:(b + 1) * P], vcols)
                    ins.then_inc(s_pair, 1)

                def rotate(n):
                    where, tile = ROPES[n]
                    o = 1024 + (n % 4) * 512
                    if n >= 4:
                        pe.wait_ge(s_roped, 11 * l + n - 3)
                    if where == 64:
                        ins = mm(ps[:, o:o + LAT], rot64, zv[:, tile, 0:LAT])
                    else:
                        x = qB[0:96, tile, 0:LAT] if where == "q" else zv[0:96, tile, 0:LAT]
                        ins = mm(ps[0:96, o:o + LAT], rot96, x)
                    ins.then_inc(s_rot, 1)

                turn(0, A_V)
                turn(1, D_V)
                rotate(0)
                pe.wait_ge(s_pn, 6 * l + 3)
                for n in range(1, 7):
                    rotate(n)
                pe.wait_ge(s_atab, 64 * (l + 1))
                pe.wait_ge(s_pn, 6 * (l + 1))
                for n in range(2, 12):
                    latent(n)
                for n in range(7, 11):
                    rotate(n)
                pe.wait_ge(s_paire, 12 * (l + 1))
                pe.wait_ge(s_roped, 11 * (l + 1))
                pe.wait_ge(s_krc, l + 1)
                pe.wait_ge(s_pads, 2 * (l + 1))
                pe.wait_ge(s_qz, l + 1)
                for n, b0 in streams(l):
                    win = b0 == 0
                    nk = NB if win else NBC
                    with pe.Fori(0, n) as i:
                        it = i + (l * NB + b0)

                        def scores(h):
                            if h >= 2:
                                pe.wait_ge(s_P, 1 + it * 12 + (h - 1))
                            else:
                                pe.wait_ge(s_P, 1 + it * 12)
                            grp, hh = h // 4, h % 4
                            o = (h % 2) * 1024
                            if grp == 1:
                                q, k, rows = qb[0:96, hh, :], kB[:, hh, :], slice(0, 96)
                            else:
                                rows = slice(0, P)
                                q = (qa, None, qd)[grp][:, hh, :]
                                k = zv[:, (A_K, None, D_K)[grp], :]
                            if win and grp == 2:
                                if hh == 0:
                                    pe.wait_ge(s_kw, i + (NBL * l + 1))
                                mm(ps[:, o:o + 384], q, kwin[rows, :])
                            elif win:
                                mm(ps[:, o:o + LAT], q, k[rows, 0:LAT])
                            oc = o + LAT if win else o
                            mm(ps[:, oc:oc + CTX], q, k[rows, LAT:TOK]).then_inc(s_S, 1)

                        def turns(h):
                            pe.wait_ge(s_P, 1 + it * 12 + (h + 1))
                            pe.wait_ge(s_pta, 1 + it * 12 + h)
                            pe.wait_ge(s_ptd, 1 + it * 12 + h)
                            for b in range(5 if win and h >= 8 else nk):
                                c = 2048 + b * (P if win else 512)
                                ins = pe.transpose(ps[:, c:c + P],
                                                   prob[:, h % 2, b * P:(b + 1) * P], ident)
                            ins.then_inc(s_T, 1)

                        def output(h):
                            pe.wait_ge(s_pta, 1 + it * 12 + (h + 1))
                            pe.wait_ge(s_ptd, 1 + it * 12 + (h + 1))
                            if h >= 2:
                                pe.wait_ge(s_on, 1 + it * 12 + (h - 1))
                            grp, hh = h // 4, h % 4
                            o = 3072 + (h % 2) * 512
                            kb = list(range(NB)) if win else list(range(NBL, NB))
                            if grp == 2 and win:
                                kb = [0, 1, 2, NBL, NBL + 1]
                            for j, b in enumerate(kb):
                                if grp == 0:
                                    v = vA[:, b, :]
                                elif grp == 1:
                                    v = vB[:, b, (hh // 2) * P:(hh // 2) * P + P]
                                elif win and j < 3:
                                    v = work[:, ds(i * P + (W_VD + j * P), P)]
                                else:
                                    v = vD[:, b + 2, :]
                                ins = mm(ps[:, o:o + P], probT[:, h % 2, j * P:(j + 1) * P], v, j == 0, j == len(kb) - 1)
                            ins.then_inc(s_O, 1)

                        pe.wait_ge(s_qt, it + 1)
                        pe.wait_ge(s_on, 1 + it * 12)
                        scores(0)
                        scores(1)
                        for h in range(12):
                            turns(h)
                            if h < 10:
                                scores(h + 2)
                            output(h)

                pe.wait_ge(s_on, 1 + (12 * (l * NB + (NB if l == 0 else NBL))))
                pe.wait_ge(s_shift, 9 * (l + 1))
                pe.wait_ge(s_gate, 2 * l + 1)
                pe.wait_ge(s_rtab, 64 * (l + 1))
                for n in range(12):
                    if n >= 2:
                        pe.wait_ge(s_rpe, 12 * l + n - 1)
                    o = (n % 2) * 1024
                    if n < 2:
                        for b in range(NB):
                            ins = pe.transpose(ps[:, o + b * P:o + (b + 1) * P], zv[:, R_V + n, b * P:(b + 1) * P], ident)
                    elif n < 4:
                        for b in (range(4) if n == 2 else range(4, 6)):
                            c = o + (b % 4) * 256
                            mm(ps[:, c:c + 256], zv[:, R_GL, b * P:(b + 1) * P], g2a, True, False)
                            ins = mm(ps[:, c:c + 256], zv[0:32, R_MISC, b * P:(b + 1) * P], g2b, False, True)
                    else:
                        rows = slice(0, 64) if n < 8 else slice(64, 128)
                        for a, b in ((0, LAT), (LAT, TOK)):
                            ins = mm(ps[:, o + a:o + b], w2a2[rows, (n % 4) * P:(n % 4 + 1) * P], zv[rows, R_WA, a:b])
                    ins.then_inc(s_rp, 1)
                for n in range(4):
                    pe.wait_ge(s_kkq, 4 * l + n + 1)
                    if n >= 2:
                        pe.wait_ge(s_kkr, 4 * l + n - 1)
                    o = 2048 + (n % 2) * 1024
                    for a, b in ((0, LAT), (LAT, TOK)):
                        ins = mm(ps[:, o + a:o + b], bd, rn[:, n, a:b])
                    ins.then_inc(s_kks, 1)
                pe.wait_ge(s_gate, 2 * l + 2)
                pe.wait_ge(s_kkr, 4 * (l + 1))
                for b in range(NB):
                    for f in range(2):
                        ins = mm(ps[:, 3584 + b * 4 + 2 * f:3586 + b * 4 + 2 * f], bonus_in[:, f, b * P:(b + 1) * P],
                                 bd[:, 0:P:64])
                ins.then_inc(s_bonps, 1)
                pe.wait_ge(s_bon, l + 1)
                pe.wait_ge(s_prep, 5 * l + 5)
                step0 = NB * l
                for n, b0 in SCAN:
                    with pe.Fori(0, n) as i:
                        it = i + step0
                        for g in range(2):
                            r, o = G[g], g * 2048
                            pe.wait_ge(s_AR[g], 1 + it + 1)
                            pe.wait_ge(s_BK[g], 1 + it + 1)
                            pe.wait_ge(s_ye[g], 1 + it)
                            pe.wait_ge(s_Sn[g], 1 + it * 2)
                            for f in range(2):
                                ins = mm(ps[:, o + 512 * f:o + 512 * f + 512], r["bt"][:, f, :],
                                         r["ar"][:, 2 * f:2 * f + 2, :, :].rearrange("p h j t -> p (h j t)"))
                            ins.then_inc(s_pre[g], 1)
                            for f in range(2):
                                ins = mm(ps[:, o + 1024 + 512 * f:o + 1536 + 512 * f], r["kt"][:, f, :],
                                         r["ar"][:, 2 * f:2 * f + 2, :, :].rearrange("p h j t -> p (h j t)"))
                            ins.then_inc(s_pre[g], 1)
                        for g in range(2):
                            r, o = G[g], g * 2048
                            pe.wait_ge(s_msk[g], it * 3 + 1)
                            for j, src in enumerate([r["ar"][:, h, 0, :] for h in range(4)] +
                                                    [r[x][:, f, :] for x in ("bt", "kt") for f in range(2)]):
                                ins = pe.transpose(ps[:, o + j * P:o + (j + 1) * P], src, ident)
                            ins.then_inc(s_pre[g], 1)
                            pe.wait_ge(s_msk[g], it * 3 + 2)
                            for h, f, rows in HEADS:
                                ins = mm(ps[:, o + 1024 + P * h:o + 1024 + P * (h + 1)], r["ar"][:, h, 0, :], r["bt"][:, f, :])
                            ins.then_inc(s_pre[g], 1)
                        for j in range(len(LEVELS)):
                            for g in range(2):
                                r, o = G[g], g * 2048
                                if j == 0:
                                    pe.wait_ge(s_msk[g], it * 3 + 3)
                                    pe.wait_ge(s_tti[g], it + 1)
                                else:
                                    pe.wait_ge(s_Tu[g], it * 9 + 2 * j)
                                for h, f, rows in HEADS:
                                    ins = mm(ps[:, o + 1536 + P * h:o + 1536 + P * (h + 1)], r["abr"][:, h, 0:P],
                                             r["t"][:, h, :])
                                ins.then_inc(s_X[g], 1)
                            for g in range(2):
                                r, o = G[g], g * 2048
                                pe.wait_ge(s_Xm[g], it * 5 + (j + 1))
                                if j == 0:
                                    pe.wait_ge(s_tok[g], it + 1)
                                if j < 4:
                                    for h, f, rows in HEADS:
                                        ins = mm(ps[:, o + P * h:o + P * (h + 1)], r["tt"][:, h, :], r["x"][:, h, :])
                                    ins.then_inc(s_Tp[g], 1)
                                for h, f, rows in HEADS:
                                    ins = mm(ps[:, o + 512 + P * h:o + 512 + P * (h + 1)], r["x"][:, h, :], r["tt"][:, h, :])
                                ins.then_inc(s_Tp[g], 1)
                        for g in range(2):
                            r, o = G[g], g * 2048
                            pe.wait_ge(s_V[g], it + 1)
                            for h, f, rows in HEADS:
                                ins = mm(ps[:, o + 1536 + P * h:o + 1536 + P * (h + 1)], r["akr"][:, h, 0:P],
                                         r["vs"][:, f * P:(f + 1) * P])
                            ins.then_inc(s_kv[g], 1)
                        for g in range(2):
                            r, o = G[g], g * 2048
                            pe.wait_ge(s_Tu[g], it * 9 + 9)
                            for h, f, rows in HEADS:
                                ins = mm(ps[:, o + 1024 + P * h:o + 1024 + P * (h + 1)], r["tok"][:, P * h:P * (h + 1)],
                                         r["tt"][:, h, :])
                            ins.then_inc(s_W[g], 1)
                            pe.wait_ge(s_kve[g], it * 2 + 1)
                            for h, f, rows in HEADS:
                                ins = mm(ps[:, o + P * h:o + P * (h + 1)], r["tt"][:, h, :],
                                         r["akv"][:, 2 * f:2 * f + 2, :].rearrange("p h i -> p (h i)"))
                            ins.then_inc(s_kv[g], 1)
                        for k in range(2):
                            for g in range(2):
                                r, o = G[g], g * 2048
                                if k == 0:
                                    pe.wait_ge(s_Wt[g], it + 1)
                                    pe.wait_ge(s_kve[g], it * 2 + 2)
                                pe.wait_ge(s_Sn[g], 1 + it * 2 + k)
                                pe.wait_ge(s_Us[g], 1 + it * 2 + k)
                                for h, f, rows in HEADS:
                                    ins = mm(ps[:, o + 512 + P * h:o + 512 + P * (h + 1)], r["wt"][:, h, :],
                                             st[g][:, f, :, :].rearrange("p s i -> p (s i)"))
                                ins.then_inc(s_U[g], 1)
                            for g in range(2):
                                r, o = G[g], g * 2048
                                c = k if g == 0 else 1 - k
                                tr = slice(64 * c, 64 * c + 64)
                                pe.wait_ge(s_Us[g], 1 + it * 2 + (k + 1))
                                pe.sem_inc(s_seen, 1)
                                for h, f, rows in HEADS:
                                    out = ps[rows, o + 1536 + 64 * f:o + 1600 + 64 * f]
                                    mm(out, r["tok"][tr, 768 + 64 * h:832 + 64 * h], r["vs"][tr, 64 * h:64 * h + 64], True, False)
                                    ins = mm(out, r["tok"][tr, 512 + 64 * h:576 + 64 * h], r["u"][tr, h, :], False, True)
                                ins.then_inc(s_dS[g], 1)
                        for g in range(2):
                            r, o = G[g], g * 2048
                            for h, f, rows in HEADS:
                                out = ps[:, o + 1024 + P * h:o + 1024 + P * (h + 1)]
                                two = [P, 2, 64]
                                mm(out, r["ar"][:, h, 1, :], st[g][:, f, :, :].rearrange("p s i -> p (s i)"), True, False)
                                mm(out, r["abr"][:, h, P:256], r["u"][:, h, :].unsqueeze(1).to_broadcast(two), False, False)
                                ins = mm(out, r["akr"][:, h, P:256],
                                         r["vs"][:, 64 * h:64 * h + 64].unsqueeze(1).to_broadcast(two), False, True)
                            ins.then_inc(s_y[g], 1)
                    step0 = step0 + n
                pe.wait_ge(s_rout, 2 * (l + 1))
                for g in range(2):
                    pe.wait_ge(s_Sn[g], 1 + 2 * NB * (l + 1))
                for f in range(KT):
                    if f >= 2:
                        pe.wait_ge(s_ote, KT * l + f - 1)
                    for b in range(nbk):
                        ins = pe.transpose(ps[:, (f % 2) * 1024 + b * P:(f % 2) * 1024 + (b + 1) * P],
                                           mix[:, b, f * P:(f + 1) * P], ident)
                    ins.then_inc(s_ot, 1)
                pe.wait_ge(s_ote, KT * (l + 1))
                with pe.Fori(0, KT // SLOTS) as i:
                    for q in range(SLOTS):
                        pe.wait_ge(s_ev, 1 + i * SLOTS + (60 * l + NZ + q - 1))
                        product(oT, (q % 2) * 1024, q, i, t).then_inc(s_tile[q], 1)
                fills[0] += KT // SLOTS
                ssq(l, 1)
                ssq(l, 2)
                pe.wait_ge(s_h, 16 * (l + 1))
                with pe.Fori(0, FFG) as i:
                    for k in range(KT):
                        q = k % SLOTS
                        pe.wait_ge(s_ev, 1 + i * KT + (60 * l + NZ + KT + k - 1))
                        pe.wait_ge(s_slab[q], i * 64 + 16 * (fills[0] + k // SLOTS + 1))
                        for a, b in ((0, LAT), (LAT, TOK)) if t == TOK else ((0, LAT),):
                            for j in range(KT):
                                ins = mm(ps[:, (k % 2) * 1024 + a:(k % 2) * 1024 + b],
                                         slab[:, q * SLAB + j * P:q * SLAB + (j + 1) * P], hv[:, j, a:b], j == 0, j == KT - 1)
                        ins.then_inc(s_tile[q], 1)
                    pe.wait_ge(s_h1, i * KT + (32 * l + KT))
                    for k in range(KT):
                        q = k % SLOTS
                        if k >= 2:
                            pe.wait_ge(s_ev2, 1 + i * KT + (32 * l + k - 1))
                        else:
                            pe.wait_ge(s_ev2, 1 + i * KT + 32 * l)
                        pe.wait_ge(s_slab[q], i * 64 + 16 * (fills[0] + 2 + k // SLOTS + 1))
                        for a, b in ((0, LAT), (LAT, TOK)) if t == TOK else ((0, LAT),):
                            for j in range(KT):
                                ins = mm(ps[:, 2048 + (k % 2) * 1024 + a:2048 + (k % 2) * 1024 + b],
                                         slab[:, q * SLAB + j * P:q * SLAB + (j + 1) * P], h1[:, j, a:b], j == 0, j == KT - 1)
                        ins.then_inc(s_tile[q], 1)
                fills[0] += 4 * FFG
                ssq(l, 3)


def constants():
    kf = np.zeros((NKF, P, P), np.float32)
    kf[K_ID] = np.eye(P)
    kf[K_ONES] = 1.0
    kf[K_BD, 0:64, 0:64] = kf[K_BD, 64:, 64:] = 1.0
    inv = {d: (np.float32(10000.0) ** (-np.arange(d // 4, dtype=np.float32) / np.float32(d // 4))).astype(np.float32)
           for d in (64, 32)}
    t = np.arange(LAT)
    place = ((t // 64).astype(np.float32), (t % 64).astype(np.float32))

    def rotation(dim, base, size, matrix, cos, sin):
        n = dim // 4
        for part in range(2):
            ang = place[part][None, :] * inv[dim][:, None]
            for half in range(2):
                at = base + part * 2 * n + half * n
                other = base + part * 2 * n + (1 - half) * n
                cos[at:at + n] = np.cos(ang)
                sin[at:at + n] = np.sin(ang)
                for j in range(n):
                    matrix[other + j, at + j] = -1.0 if half == 0 else 1.0

    rope = np.zeros((4, P, LAT), np.float32)
    rope[2] = 1.0
    for base in (0, 64):
        rotation(64, base, P, kf[K_ROT64], rope[0], rope[1])
    rotation(32, 64, 96, kf[K_ROT96], rope[2], rope[3])

    row, col = np.arange(P)[:, None], np.arange(P)[None, :]
    same = (row // CH) == (col // CH)
    km = []
    for g in range(2):
        before = (lambda a, b: a < b) if g == 0 else (lambda a, b: a > b)
        km.append(same & before(row, col))
        km.append(same & (before(row, col) | (row == col)))
        first = (row // 2 == col // 2) & before(col, row)
        km += [first, first.T]
        for h in LEVELS:
            km.append((row // (2 * h) == col // (2 * h)) & (row // h != col // h) & before(col, row))
    km = np.stack(km).astype(np.float32)

    wmask = np.full((NBL, P, 384), NEG, np.float32)
    key = np.arange(384)[None, :] - P
    for b in range(NBL):
        at = b * P + key
        wmask[b][(np.abs(row - key) <= P) & (at >= 0) & (at < LAT)] = 0.0
    smask = np.ones((P, TOK), np.float32)
    smask[:, ::CH] = 0.0
    return (kf.transpose(1, 0, 2).reshape(P, -1), km.transpose(1, 0, 2).reshape(P, -1),
            rope.transpose(1, 0, 2), wmask.transpose(1, 0, 2), smask)


def kernel(**inputs):
    import concourse.bacc as bacc
    from concourse.bass_utils import run_bass_kernel_spmd

    a = {k: np.asarray(v) for k, v in inputs.items()}
    L = DEPTH

    def tiles(v):
        return v.reshape(L, -1, P).transpose(0, 2, 1)

    def slabs(w):
        n = w.shape[2] // P
        return w.reshape(L, KT, P, n, P).transpose(0, 3, 2, 1, 4).reshape(L * n, P, KT * P)

    ga, gb, gc, gd = 0, 512, 928, 1984
    heads = lambda at: [np.arange(at + (2 * g + r) * 64, at + (2 * g + r) * 64 + 64) for r in range(2) for g in range(2)]
    cols = [*heads(ga), np.arange(ga + 256, ga + 512), *heads(gd), np.arange(gd + 256, gd + 512),
            np.arange(gb, gb + 384), np.arange(gc, gc + 1024), np.arange(gc + 1024, gc + 1056), np.full(32, -1),
            np.arange(gb + 384, gb + 416), np.full(32, -1)]
    cols = np.concatenate(cols)
    w_in = np.concatenate([a["w_in"], np.zeros((L, DM, 1), np.float32)], axis=2)[:, :, cols]
    mu = np.concatenate([a["rwkv_mu"], np.zeros((L, 96), np.float32)], axis=1)
    mod = a["w_mod"].reshape(L, SLOTS, 2, P, 12, 512).transpose(0, 4, 1, 3, 2, 5).reshape(L * NMOD, P, 1024)
    pcol = np.concatenate([
        tiles(a["b_mod"]), tiles(a["g_pre_mix"]), tiles(a["g_post_mix"]), tiles(a["g_pre_mlp"]), tiles(a["g_post_mlp"]),
        tiles(np.tile(a["gqa_q_norm"], (1, 2))), tiles(np.tile(a["gqa_k_norm"], (1, 2))), tiles(a["mla_q_norm"]),
        tiles(a["mla_kv_norm"]), tiles(mu), tiles(a["rwkv_w0"].reshape(L, -1)), tiles(a["rwkv_a0"].reshape(L, -1)),
        tiles(a["rwkv_k_k"].reshape(L, -1)), tiles(a["rwkv_k_a"].reshape(L, -1)), tiles(a["rwkv_r_k"].reshape(L, -1)),
        np.broadcast_to(a["swa_sink"][:, None, :], (L, P, 4))], axis=2)
    kf, km, rope, wmask, smask = constants()
    g2 = np.zeros((L, P, 512), np.float32)
    g2[:, :, 0:256] = a["rwkv_g2"][:, 0:P]
    g2[:, 0:32, 256:512] = a["rwkv_g2"][:, P:160]
    w2a2 = np.concatenate([a["rwkv_w2"].transpose(0, 2, 1, 3).reshape(L, 64, 512),
                           a["rwkv_a2"].transpose(0, 2, 1, 3).reshape(L, 64, 512)], axis=1)
    tokens = np.concatenate([a["x"][0], a["ctx"][0]], axis=0)
    data = {
        "xT": tokens.T.reshape(KT, P, TOK).transpose(1, 0, 2),
        "cT": np.stack([a["c"][0], a["c_ctx"]], axis=1).reshape(KT, P, 2).transpose(1, 0, 2).reshape(P, KT * 2),
        "pcol": pcol, "constf": kf, "constm": km, "rope": rope, "wmask": wmask,
        "wmod": mod, "win": slabs(w_in), "wout": slabs(a["w_out"]), "w1": slabs(a["w_mlp1"]),
        "w2": a["w_mlp2"].reshape(L, FFG, KT, P, KT, P).transpose(0, 1, 4, 3, 2, 5).reshape(L * FFG * KT, P, DM),
        "uq": a["mla_w_uq"].reshape(L, 2, P, 384).transpose(0, 2, 1, 3),
        "ukv": a["mla_w_ukv"], "w2a2": w2a2, "g2": g2,
        "ln": np.broadcast_to(np.concatenate([a["rwkv_ln_w"], a["rwkv_ln_b"]], axis=1)[:, None, :], (L, P, 512)),
        "smask": smask,
    }
    data = {k: np.ascontiguousarray(v) for k, v in data.items()}
    nc = bacc.Bacc("TRN2", target_bir_lowering=False, num_devices=1)
    args = [nc.dram_tensor(f"{k}_dram", v.shape, mybir.dt.from_np(v.dtype), kind="ExternalInput").ap() for k, v in data.items()]
    args.append(nc.dram_tensor("out_dram", (P, KT, LAT), F32, kind="ExternalOutput").ap())
    backbone(nc, *args)
    r = run_bass_kernel_spmd(nc, [{f"{k}_dram": v for k, v in data.items()}], core_ids=[0])
    got = r.results[0]["out_dram"]
    return got.transpose(1, 0, 2).reshape(DM, LAT).T.reshape(1, LAT, DM)
```

```python
from contextlib import ExitStack

import concourse.bass as bass
from concourse import mybir
import numpy as np

ALU = mybir.AluOpType
ACT = mybir.ActivationFunctionType
AX = mybir.AxisListType
F32 = mybir.dt.float32
BF16 = mybir.dt.bfloat16
F32R = mybir.dt.float32r
ds = bass.ds

P = 128
DM = 1024
KT = DM // P
LAT = 512
CTX = 256
TOK = LAT + CTX
NBL, NBC = LAT // P, CTX // P
NB = NBL + NBC
DEPTH = 2
NZ = 20
NMOD = 48
SLOTS = 4
SLAB = 1024
FFG = 4
F_IN = NMOD // SLOTS
F_OUT = F_IN + NZ // SLOTS
F_MLP = F_OUT + KT // SLOTS
FILLS = F_MLP + 2 * FFG * KT // SLOTS
T_OUT = NZ // SLOTS
T_MLP = T_OUT + KT // SLOTS
TILES = T_MLP + 2 * FFG * KT // SLOTS
EPS = 1e-6
GN_EPS = 64e-5
DECAY = 0.6065306597126334
CH = 64
LEVELS = (2, 4, 8, 16, 32)
NEG = -1e30

A_Q, A_K, A_V, D_Q, D_K, D_V, C_Q, C_KV = 0, 2, 3, 4, 6, 7, 8, 10
R_R, R_K, R_V, R_WA, R_GL, R_MISC = 11, 13, 15, 17, 18, 19

PC = {}
_at = 0
for _name, _n in (("b_mod", 48), ("g_pre_mix", 8), ("g_post_mix", 8), ("g_pre_mlp", 8), ("g_post_mlp", 8),
                  ("q_norm", 1), ("k_norm", 1), ("cq_norm", 2), ("ckv_norm", 1), ("mu", 9), ("w0", 4), ("a0", 4),
                  ("k_k", 4), ("k_a", 4), ("r_k", 2), ("sink", 4)):
    PC[_name] = _at
    _at += _n
NPC = _at

K_ID, K_ONES, K_BD, K_ROT64, K_ROT96 = range(5)
NKF = 5
MASKS_DIR = 2 + 2 + len(LEVELS)
NKM = 2 * MASKS_DIR

W_QB, W_KB, W_VB, W_VA, W_VD = 0, 3072, 6144, 7680, 8448
W_ROPE, W_WMASK, W_UQ, W_UKV = 9472, 11520, 13056, 13824
W_P, W_PT, W_QT = 14336, 15872, 17408
W_KD, W_G, W_LN = 0, 3072, 17920
W_SCR, SCR = 4608, 6144
W_W2A2, W_G2A, W_G2B, W_SMASK, W_SG, W_A, W_RN = 6400, 7424, 7680, 7936, 8704, 11776, 14848
W_ST = W_SCR + 2 * SCR
WORK = 18432
W_HI, W_LO, W_SPLIT = 0, KT * TOK, 14336


def backbone(nc, xT_d, cT_d, pcol_d, constf_d, constm_d, rope_d, wmask_d, wmod_d, win_d, wout_d, w1_d, w2_d,
             uq_d, ukv_d, w2a2_d, g2_d, ln_d, smask_d, out_d):
    with ExitStack() as ctx:
        place = {}

        def sb(name, cols, dt=F32):
            place[name] = nc.sbuf_base
            return ctx.enter_context(nc.sbuf_tensor(name, [P, cols], dt))

        def sem(name):
            return ctx.enter_context(nc.semaphore(name))

        xT = sb("xT", KT * TOK)
        hT = sb("hT", KT * TOK)
        zT = sb("zT", NZ * TOK)
        slab = sb("slab", SLOTS * SLAB)
        work = sb("work", WORK)
        pcol = sb("pcol", DEPTH * NPC)
        kf = sb("kf", NKF * P)
        km = sb("km", NKM * P, BF16)
        cT = sb("cT", KT * 2)
        silu = sb("silu", KT * 2)
        modT = sb("modT", NMOD * 2)
        gain = sb("gain", 4 * 16)
        omm = sb("omm", 32)
        small = sb("small", 96)
        bon = sb("bon", NB * 4)
        eps = sb("eps", 1)
        ps = ctx.enter_context(nc.psum_tensor("ps", [P, 4096], F32))

        xv = xT[:, :].rearrange("p (k t) -> p k t", k=KT)
        hv = hT[:, :].rearrange("p (k t) -> p k t", k=KT)
        zv = zT[:, :].rearrange("p (k t) -> p k t", k=NZ)
        mv = modT[:, :].rearrange("p (k s) -> p k s", s=2)
        gv = gain[:, :].rearrange("p (n k s) -> p n k s", n=4, s=2)
        ident, ones, bd = (kf[:, k * P:(k + 1) * P] for k in (K_ID, K_ONES, K_BD))
        rot64 = kf[:, K_ROT64 * P:(K_ROT64 + 1) * P]
        rot96 = kf[0:96, K_ROT96 * P:K_ROT96 * P + 96]
        modrow = work[0:2, 0:NMOD * P]

        def wv(at, *dims):
            n = int(np.prod(dims))
            if len(dims) == 1:
                return work[:, at:at + n]
            if len(dims) == 2:
                return work[:, at:at + n].rearrange("p (a b) -> p a b", a=dims[0])
            return work[:, at:at + n].rearrange("p (a b c) -> p a b c", a=dims[0], b=dims[1])

        qB, kB = wv(W_QB, 4, TOK), wv(W_KB, 4, TOK)
        vB, vA = wv(W_VB, NB, 256), wv(W_VA, NB, P)
        vD = wv(W_VD, 8, P)
        rope = wv(W_ROPE, 4, LAT)
        wmask = wv(W_WMASK, NBL, 384)
        uq, ukv = wv(W_UQ, 2, 384), wv(W_UKV, 512)
        prob, probT = wv(W_P, 2, TOK), wv(W_PT, 2, TOK)
        qa, qd = (zT[:, t * TOK:t * TOK + 4 * P].rearrange("p (h t) -> p h t", h=4) for t in (C_Q, C_Q + 1))
        qb = wv(W_QT, 4, P)
        kwin = zT[:, C_KV * TOK:C_KV * TOK + 384]
        mix = hT[:, :].rearrange("p (b f) -> p b f", b=NB)

        def parts(name, over, at, cols):
            return nc.alloc_sbuf_tensor_at(name, [P, cols], F32R, offset=place[over] + 4 * at)

        wparts = parts("wparts", "work", W_SPLIT, 4 * SLAB)
        whi = [wparts[:, q * SLAB:(q + 1) * SLAB] for q in range(2)]
        wlo = [wparts[:, (2 + q) * SLAB:(3 + q) * SLAB] for q in range(2)]
        part_hi, part_lo, part_h, part_mlp = (
            parts(name, over, at, KT * TOK)[:, :].rearrange("p (k t) -> p k t", k=KT)
            for name, over, at in (("part_hi", "work", W_HI), ("part_lo", "work", W_LO), ("part_h", "hT", 0),
                                   ("part_mlp", "zT", KT * TOK)))
        pre_hi, pre_lo = (part_hi, None, part_mlp), part_h
        o_hi, o_lo = part_hi, part_lo
        h1_hi, h1_lo = o_hi, o_lo
        h1 = zv[:, 2 * KT:2 * KT + 2, :]
        yT = zv[:, 0:KT, :]
        sq = zv[:, KT:2 * KT, :]
        NS, RS = 3400, 2560
        rs = ps[:, RS:RS + TOK]
        rcol = small[:, 80:80 + NB]
        AS, ASPREAD = 2900, (1024, 2048, 0, 3072, 1024)
        KS, BONUS = 3844, 3900
        kd, gtok = wv(W_KD, 4, TOK), wv(W_G, NB, 256)
        lnw, lnb = wv(W_LN, 256), wv(W_LN + 256, 256)
        nkk, bh, cs = zv[:, 0:4, :], zv[:, 4:8, :], zv[:, 15:19, :]
        vtok = zT[:, 8 * TOK:10 * TOK].rearrange("p (b f) -> p b f", b=NB)
        bonus_in = zv[:, R_K:R_K + 2, :]
        yrev = zT[:, R_K * TOK:(R_K + 2) * TOK].rearrange("p (b f) -> p b f", b=NB)
        w2a2, g2a, g2b = wv(W_W2A2, 1024), wv(W_G2A, 256), work[0:32, W_G2B:W_G2B + 256]
        smask = wv(W_SMASK, TOK)
        sg, aa, rn = wv(W_SG, 4, TOK), wv(W_A, 4, TOK), wv(W_RN, 4, TOK)

        G = []
        for g in range(2):
            o = W_SCR + g * SCR
            G.append(dict(
                ar=wv(o, 4, 2, P),
                bt=wv(o + 1024, 2, P), kt=wv(o + 1280, 2, P), ei=wv(o + 1536, 2, P),
                x=wv(o + 1024, 4, P),
                uv=wv(o + 1024, 4, 64),
                akv=wv(o + 1536, 4, 64),
                ep=sb(f"decay{g}", 260)[:, :].rearrange("p (f c t) -> p f c t", f=2, c=2),
                tok=wv(o + 1792, 1024),
                vs=wv(o + 2816, 256), abr=wv(o + 3072, 4, 256), akr=wv(o + 4096, 4, 256),
                t=wv(o + 5120, 4, P), tt=wv(o + 5632, 4, P),
                wt=wv(o + 5120, 4, P)))
        for g in range(2):
            G[g]["u"] = zT[:, 10 * TOK + g * 256:10 * TOK + g * 256 + 256].rearrange("p (h i) -> p h i", h=4)
        st = [wv(W_ST + g * 256, 2, 2, 64) for g in range(2)]
        s1 = [wv(W_ST + 512 + g * P, 2, 64) for g in range(2)]

        def mask(g, k, n=1):
            o = (g * MASKS_DIR + k) * P
            return km[:, o:o + n * P]

        s_const = sem("s_const")
        s_x = sem("s_x")
        s_maskraw = sem("s_maskraw")
        s_masks = sem("s_masks")
        s_slab = [sem(f"s_slab{q}") for q in range(SLOTS)]
        s_used = [sem(f"s_used{q}") for q in range(SLOTS)]
        s_tile = [sem(f"s_tile{q}") for q in range(SLOTS)]
        s_silu = sem("s_silu")
        s_modps = sem("s_modps")
        s_modrow = sem("s_modrow")
        s_modT = sem("s_modT")
        s_eps = sem("s_eps")
        s_sq = sem("s_sq")
        s_ssq = sem("s_ssq")
        s_acc = sem("s_acc")
        s_rec = sem("s_rec")
        s_rs = sem("s_rs")
        s_rt = sem("s_rt")
        s_xn = sem("s_xn")
        s_h = sem("s_h")
        s_hlo = sem("s_hlo")
        s_xup = sem("s_xup")
        s_ev = sem("s_ev")
        s_ev2 = sem("s_ev2")
        s_h1 = sem("s_h1")
        s_dve = sem("s_dve")
        s_pool = sem("s_pool")
        s_atab = sem("s_atab")
        s_psq = sem("s_psq")
        s_pss = sem("s_pss")
        s_prt = sem("s_prt")
        s_prec = sem("s_prec")
        s_psp = sem("s_psp")
        s_pn = sem("s_pn")
        s_pair = sem("s_pair")
        s_paire = sem("s_paire")
        s_rot = sem("s_rot")
        s_roped = sem("s_roped")
        s_pads = sem("s_pads")
        s_krc = sem("s_krc")
        s_qa = sem("s_qa")
        s_qt = sem("s_qt")
        s_qz = sem("s_qz")
        s_kw = sem("s_kw")
        s_S = sem("s_S")
        s_nm = sem("s_nm")
        s_P = sem("s_P")
        s_es = sem("s_es")
        s_T = sem("s_T")
        s_pta = sem("s_pta")
        s_ptd = sem("s_ptd")
        s_O = sem("s_O")
        s_on = sem("s_on")
        s_rtab = sem("s_rtab")
        s_ln = sem("s_ln")
        s_shift = sem("s_shift")
        s_gate = sem("s_gate")
        s_rp = sem("s_rp")
        s_rpe = sem("s_rpe")
        s_kk = sem("s_kk")
        s_kkq = sem("s_kkq")
        s_kks = sem("s_kks")
        s_kkr = sem("s_kkr")
        s_krec = sem("s_krec")
        s_ksp = sem("s_ksp")
        s_kkn = sem("s_kkn")
        s_prep = sem("s_prep")
        s_bonin = sem("s_bonin")
        s_bonps = sem("s_bonps")
        s_bon = sem("s_bon")

        def pair(name):
            return [sem(f"{name}{g}") for g in range(2)]

        s_E, s_AR, s_BK, s_V = pair("s_E"), pair("s_AR"), pair("s_BK"), pair("s_V")
        s_pre, s_msk, s_tti, s_tok = pair("s_pre"), pair("s_msk"), pair("s_tti"), pair("s_tok")
        s_X, s_Xm, s_Tp, s_Tu = pair("s_X"), pair("s_Xm"), pair("s_Tp"), pair("s_Tu")
        s_Tt, s_Tte = pair("s_Tt"), pair("s_Tte")
        s_W, s_Wt, s_kv, s_kve = pair("s_W"), pair("s_Wt"), pair("s_kv"), pair("s_kve")
        s_U, s_Us, s_dS, s_Sn, s_y, s_ye = pair("s_U"), pair("s_Us"), pair("s_dS"), pair("s_Sn"), pair("s_y"), pair("s_ye")
        s_whi = sem("s_whi")
        s_seen = sem("s_seen")
        s_sawslab = sem("s_sawslab")
        s_rout = sem("s_rout")
        s_ot = sem("s_ot")
        s_ote = sem("s_ote")
        s_otl = sem("s_otl")
        s_out = sem("s_out")

        def streams(l):
            return ((NBL, 0), (NBC, NBL)) if l < DEPTH - 1 else ((NBL, 0),)

        SQ = 3 * KT

        SCAN = ((NBC, NBL), (NBL, 0))

        def segs(l, mixed):
            if l == DEPTH - 1 and mixed:
                return ((0, 0, LAT),)
            return ((0, 0, LAT), (1, LAT, TOK))

        class Chain:

            def __init__(self, eng, s):
                self.eng, self.s, self.n, self.i, self.per, self.mark = eng, s, 0, None, 0, 0

            def link(self, ins):
                ins.then_inc(self.s, 1)
                self.n += 1
                if self.i is None:
                    self.eng.wait_ge(self.s, self.n)
                else:
                    self.eng.wait_ge(self.s, self.i * self.per + self.n)

            def enter(self, i, per):
                self.i, self.per, self.mark = i, per, self.n

            def leave(self, trips):
                assert self.n - self.mark == self.per, (self.n - self.mark, self.per)
                self.n = self.mark + trips * self.per
                self.i = None

        ROPES = [("kr", R_MISC)] + [(64, tile) for tile in (A_Q, A_Q + 1, A_K, D_Q, D_Q + 1, D_K)] + [("q", h) for h in range(4)]

        HEADS = [(h, h // 2, slice(64 * (h % 2), 64 * (h % 2) + 64)) for h in range(4)]

        def own_half(o, half):
            return ps[:, o:o + 512].rearrange("p (f c) -> p f c", f=2)[:, :, half * 192:half * 192 + 64]

        block = ctx.enter_context(nc.Block())

        @block.sync
        def _(sp):
            sp.dma_start(cT[:, :], cT_d).then_inc(s_const, 16)
            sp.dma_start(pcol[:, :].rearrange("p (l n) -> p l n", l=DEPTH),
                         pcol_d.rearrange("l p n -> p l n")).then_inc(s_const, 16)
            sp.dma_start(kf[:, :], constf_d).then_inc(s_const, 16)
            used = [0]

            def stream(src, first, n):
                with sp.Fori(0, n // SLOTS) as i:
                    for q in range(SLOTS):
                        sp.wait_ge(s_used[q], 1 + used[0] + i)
                        sp.dma_start(slab[:, q * SLAB:(q + 1) * SLAB],
                                     src[ds(first + i * SLOTS + q, 1), :, :].rearrange("a p n -> (a p) n")
                                     ).then_inc(s_slab[q], 16)
                used[0] += n // SLOTS

            for l in range(DEPTH):
                stream(wmod_d, l * NMOD, NMOD // 4)
                if l == 0:
                    for k in range(KT):
                        sp.dma_start(xv[:, k, :], xT_d[:, k, :]).then_inc(s_x, 16)
                stream(wmod_d, l * NMOD + NMOD // 4, 3 * NMOD // 4)
                if l == 0:
                    sp.dma_start(zT[:, 0:NKM * P], constm_d).then_inc(s_maskraw, 16)
                stream(win_d, l * NZ, NZ)
                stream(wout_d, l * KT, KT)
                with sp.Fori(0, FFG) as i:
                    for half, src in ((0, w1_d), (1, w2_d)):
                        for k in range(KT):
                            q = k % SLOTS
                            sp.wait_ge(s_used[q], 1 + i * 4 + (used[0] + 2 * half + k // SLOTS))
                            sp.dma_start(slab[:, q * SLAB:(q + 1) * SLAB],
                                         src[ds(i * KT + (l * FFG * KT + k), 1), :, :].rearrange("a p n -> (a p) n")
                                         ).then_inc(s_slab[q], 16)
                used[0] += 4 * FFG
            for k in range(KT):
                sp.wait_ge(s_xup, DEPTH * 2 * KT - KT + k + 1)
                sp.dma_start(out_d[:, k, :], xv[:, k, 0:LAT]).then_inc(s_out, 16)
            sp.wait_ge(s_out, 16 * KT)

        @block.gpsimd
        def _(pool):
            ch = Chain(pool, s_pool)
            for first in (s_S, s_ev, s_ev2, s_modrow, s_P, s_pta, s_ptd, s_on, s_h1, *s_used, *s_tile, *s_y, *s_kv, *s_Sn, *s_AR, *s_BK,
                          *s_ye, *s_Us):
                pool.sem_inc(first, 1)

            def split(q, fill, tile, hi_done=None):
                src = slab[:, q * SLAB:(q + 1) * SLAB]
                if hi_done is None:
                    pool.wait_ge(s_slab[q], (fill + 1) * 16)
                    pool.wait_ge(s_tile[(q - 2) % SLOTS], tile + (2 if q >= 2 else 1))
                    pool.sem_inc(s_sawslab, 1)
                    ch.link(pool.tensor_copy(whi[q % 2], src))
                else:
                    pool.wait_ge(s_whi, hi_done)
                pool.tensor_tensor(wlo[q % 2], src, whi[q % 2], ALU.subtract).then_inc(s_used[q], 1)

            def splits(n, per, fill, tile, hi=None):
                with pool.Fori(0, n) as i:
                    ch.enter(i, per * SLOTS if hi is None else 2)
                    for j in range(per):
                        for q in range(SLOTS):
                            k = j * SLOTS + q
                            done = None if hi is None or k < 2 else i * (2 * KT - 2) + (hi + k - 1)
                            split(q, i * per + (fill + j), i * per + (tile + j), done)
                    ch.leave(n)

            def sum_squares(l, which):
                t = TOK if l < DEPTH - 1 else LAT
                for k in range(1, KT):
                    pool.wait_ge(s_sq, SQ * l + (which - 1) * KT + k + 1)
                    ins = pool.tensor_tensor(sq[:, 0, 0:t], sq[:, 0, 0:t], sq[:, k, 0:t], ALU.add)
                    if k < KT - 1:
                        ch.link(ins)
                ins.then_inc(s_acc, 1)

            for l in range(DEPTH):
                pool.wait_ge(s_modT, l + 1)
                for dst, src in ((rope, rope_d), (wmask, wmask_d), (uq, uq_d[l]), (ukv, ukv_d[l])):
                    pool.dma_start(dst, src).then_inc(s_atab, 16)
                pool.memset(vD[:, 0, :], 0.0)
                pool.memset(vD[:, 5, :], 0.0).then_inc(s_pads, 1)
                splits(NZ // SLOTS, 1, FILLS * l + F_IN, TILES * l)
                pool.wait_ge(s_pair, 12 * l + 2)
                pool.memset(zv[:, D_V, 0:P], 0.0)
                pool.memset(zv[:, D_V, P + LAT:TOK], 0.0).then_inc(s_pads, 1)
                pool.wait_ge(s_pair, 12 * (l + 1))
                pool.wait_ge(s_roped, 11 * l + 7)
                pool.wait_ge(s_pads, 2 * (l + 1))
                nbs = zv[:, A_V, :]
                for i in range(NBL):
                    pool.wait_ge(s_S, 1 + (l * NB + i) * 12)
                    pool.tensor_copy(kwin, zv[:, D_V, i * P:i * P + 384]).then_inc(s_kw, 1)
                    for k in range(9)[i * 3:i * 3 + 3]:
                        z = zv[:, R_R + k, :]
                        ch.link(pool.tensor_tensor(nbs[:, 1:TOK - 1], z[:, 0:TOK - 2], z[:, 2:TOK], ALU.add))
                        pool.tensor_copy(nbs[:, 0:1], z[:, 1:2])
                        pool.tensor_copy(nbs[:, TOK - 1:TOK], z[:, TOK - 2:TOK - 1])
                        pool.tensor_copy(nbs[:, LAT - 1:LAT], z[:, LAT - 2:LAT - 1])
                        ch.link(pool.tensor_copy(nbs[:, LAT:LAT + 1], z[:, LAT + 1:LAT + 2]))
                        pool.tensor_tensor(z, z, omm[:, k:k + 1].to_broadcast([P, TOK]), ALU.mult)
                        ch.link(pool.tensor_tensor(nbs, nbs, omm[:, 9 + k:10 + k].to_broadcast([P, TOK]), ALU.mult))
                        ch.link(pool.tensor_tensor(z, z, nbs, ALU.add))
                pool.sem_inc(s_shift, 1)

                pool.wait_ge(s_on, 1 + 12 * (l * NB + (NB if l == 0 else NBL)))
                for i, (dst, src) in enumerate(((w2a2, w2a2_d[l]), (g2a, g2_d[l, :, 0:256]), (g2b, g2_d[l, 0:32, 256:512]),
                                                (smask, smask_d))):
                    pool.dma_start(dst, src).then_inc(s_rtab, 16)
                pool.wait_ge(s_shift, l + 1)
                pool.dma_start(lnw, ln_d[l, :, 0:256]).then_inc(s_ln, 16)
                pool.dma_start(lnb, ln_d[l, :, 256:512]).then_inc(s_ln, 16)
                pool.wait_ge(s_prep, 5 * l + 4)
                for f in range(2):
                    ch.link(pool.tensor_tensor(bonus_in[:, f, :], kd[:, f, :], kd[:, 2 + f, :], ALU.add))
                    pool.tensor_tensor(bonus_in[:, f, :], bonus_in[:, f, :], zv[:, R_R + f, :],
                                       ALU.mult).then_inc(s_bonin, 1)

                pool.wait_ge(s_prep, 5 * l + 5)
                step0 = NB * l
                for n, b0 in SCAN:
                    with pool.Fori(0, n) as i:
                        ch.enter(i, 2)
                        for g in range(2):
                            r = G[g]
                            off = i * P + b0 * P if g == 0 else i * (-P) + (b0 + n - 1) * P
                            vof = i * 256 + b0 * 256 if g == 0 else i * (-256) + (b0 + n - 1) * 256
                            pool.wait_ge(s_E[g], i + (step0 + 1))
                            pool.wait_ge(s_y[g], 1 + i + step0)
                            pool.tensor_tensor(r["bt"], bh[:, 2 * g:2 * g + 2, ds(off, P)], r["ei"], ALU.mult)
                            pool.tensor_tensor(r["kt"], kd[:, 2 * g:2 * g + 2, ds(off, P)], r["ei"],
                                               ALU.mult).then_inc(s_BK[g], 1)
                            pool.tensor_copy(r["vs"], zT[:, ds(vof + 8 * TOK, 256)]).then_inc(s_V[g], 1)
                        for g in range(2):
                            r = G[g]
                            pool.wait_ge(s_msk[g], (i + step0) * 3 + 1)
                            pool.wait_ge(s_kv[g], 1 + (i + step0) * 2)
                            ch.link(pool.tensor_tensor(
                                r["tt"], r["abr"][:, :, 0:P],
                                mask(g, 3).unsqueeze(1).to_broadcast([P, 4, P]), ALU.mult))
                            pool.tensor_tensor(r["tt"], r["tt"], ident.unsqueeze(1).to_broadcast([P, 4, P]),
                                               ALU.add).then_inc(s_tti[g], 1)
                        ch.leave(n)
                    step0 = step0 + n
                pool.wait_ge(s_rout, 2 * (l + 1))
                splits(KT // SLOTS, 1, FILLS * l + F_OUT, TILES * l + T_OUT)
                sum_squares(l, 2)
                splits(FFG, 4, FILLS * l + F_MLP, TILES * l + T_MLP, FFG * (2 * KT - 2) * l)
                sum_squares(l, 3)

        @block.scalar
        def _(act):
            nc_ = nc.scalar

            def par(l, name, k=0):
                return pcol[:, l * NPC + PC[name] + k:l * NPC + PC[name] + k + 1]

            act.wait_ge(s_const, 48)
            act.wait_ge(s_eps, 1)
            nc_.activation(silu[:, :], cT[:, :], ACT.Sigmoid).then_inc(s_silu, 1)

            def squares(l, which, src):
                t = TOK if l < DEPTH - 1 else LAT
                for k in range(KT):
                    if which == 2:
                        act.wait_ge(s_xup, 16 * l + k + 1)
                    else:
                        act.wait_ge(s_ev2, 1 + 32 * l + 24 + k + 1)
                    nc_.activation(sq[:, k, 0:t], src[:, k, 0:t], ACT.Square).then_inc(s_sq, 1)

            def root(n, nb):
                act.wait_ge(s_ssq, n + 1)
                nc_.activation(rcol[:, 0:nb], ps[:, NS:NS + nb], ACT.Sqrt, scale=1.0 / DM,
                               bias=eps[:, 0:1]).then_inc(s_rt, 1)

            def first_parts(l, which):
                for k in range(KT):
                    act.wait_ge(s_xn, 16 * l + 4 * which + k + 1)
                    if which == 0:
                        ins = nc_.activation(pre_hi[0][:, k, :], hv[:, k, :], ACT.Copy)
                    else:
                        for s, a, b in segs(l, True):
                            ins = nc_.activation(pre_hi[2][:, k, a:b], hv[:, k, a:b], ACT.Identity,
                                                 bias=mv[:, 24 + k, s:s + 1])
                    ins.then_inc(s_h, 1)

            for l in range(DEPTH):
                def modulation(first):
                    with act.Fori(0, 6) as i:
                        act.wait_ge(s_used[3], 1 + i + (FILLS * l + first + 1))
                        nc_.activation(work[0:2, ds(i * 512 + first * 512, 512)], ps[0:2, 3584:4096],
                                       ACT.Copy).then_inc(s_modrow, 1)

                modulation(0)
                root(4 * l, NB)
                modulation(6)
                first_parts(l, 0)
                act.wait_ge(s_masks, 1)
                with act.Fori(0, NZ // SLOTS) as i:
                    for q in range(SLOTS):
                        act.wait_ge(s_tile[q], 1 + i + (TILES * l + 1))
                        nc_.activation(zT[:, ds(i * (SLOTS * TOK) + q * TOK, TOK)],
                                       ps[:, (q % 2) * 1024:(q % 2) * 1024 + TOK], ACT.Copy).then_inc(s_ev, 1)
                act.wait_ge(s_ev, 1 + 60 * l + NZ)
                for n, tile in enumerate((A_Q, A_Q + 1, A_K, C_Q, C_Q + 1, C_KV)):
                    nc_.activation(work[:, n * TOK:(n + 1) * TOK], zv[:, tile, :], ACT.Square).then_inc(s_psq, 1)
                act.wait_ge(s_pss, l + 1)
                for width, a, b in ((64, 0, 36), (256, 36, 42), (128, 42, 48)):
                    ins = nc_.activation(small[:, a:b], ps[:, AS + a:AS + b], ACT.Sqrt, scale=1.0 / width, bias=eps[:, 0:1])
                ins.then_inc(s_prt, 1)
                for n in range(12):
                    act.wait_ge(s_pair, 12 * l + n + 1)
                    o = (n % 2) * 3072
                    if n == 0:
                        ins = nc_.activation(wv(W_VA, TOK), ps[:, o:o + TOK], ACT.Copy)
                    elif n == 1:
                        nc_.activation(wv(W_VD + P, LAT), ps[:, o:o + LAT], ACT.Copy)
                        ins = nc_.activation(wv(W_VD + 6 * P, CTX), ps[:, o + LAT:o + TOK], ACT.Copy)
                    elif n < 6:
                        ins = nc_.activation(qB[0:96, n - 2, :], ps[0:96, o:o + TOK], ACT.Copy)
                    elif n < 10:
                        ins = nc_.activation(kB[0:64, n - 6, :], ps[0:64, o:o + TOK], ACT.Copy)
                    elif n == 10:
                        ins = nc_.activation(wv(W_VB, 1024), ps[:, o:o + 1024], ACT.Copy)
                    else:
                        ins = nc_.activation(wv(W_VB + 1024, 512), ps[:, o:o + 512], ACT.Copy)
                    ins.then_inc(s_paire, 1)
                act.wait_ge(s_roped, 11 * l + 1)
                nc_.activation(kB[64:96], zv[64:96, R_MISC, :].unsqueeze(1).to_broadcast([32, 4, TOK]),
                               ACT.Copy).then_inc(s_krc, 1)
                act.wait_ge(s_roped, 11 * (l + 1))
                for n, b0 in streams(l):
                    nk = NB if b0 == 0 else NBC
                    with act.Fori(0, n) as i:
                        it = i + (l * NB + b0)
                        off = i * P + b0 * P
                        act.wait_ge(s_S, 1 + it * 12)
                        for q, tile, done in ((qa, A_Q, s_qa), (qd, D_Q, None)):
                            for g in range(2):
                                rows = slice(64 * g, 64 * g + 64)
                                ins = nc_.activation(q[rows, 2 * g:2 * g + 2, :], zv[rows, tile:tile + 2, ds(off, P)],
                                                     ACT.Copy, scale=0.125)
                            if done:
                                ins.then_inc(done, 1)
                        nc_.activation(qb[0:96], qB[0:96, :, ds(off, P)], ACT.Copy, scale=96.0 ** -0.5).then_inc(s_qt, 1)

                        def exps(h):
                            act.wait_ge(s_nm, it * 12 + (h + 1))
                            masked = h >= 8 and b0 == 0
                            w = 640 if masked else nk * P
                            if h >= 2:
                                act.wait_ge(s_T, it * 12 + (h - 1))
                            src = prob[:, h % 2, 0:w] if masked else ps[:, (h % 2) * 1024:(h % 2) * 1024 + w]
                            nc_.activation(prob[:, h % 2, 0:w], src, ACT.Exp, bias=small[:, h:h + 1],
                                           accum_out=small[:, 16 + h:17 + h]).then_inc(s_P, 1)
                            if h >= 8:
                                nc_.activation(small[:, 32 + h:33 + h], par(l, "sink", h - 8), ACT.Exp,
                                               bias=small[:, h:h + 1]).then_inc(s_es, 1)

                        def turned(h):
                            act.wait_ge(s_T, it * 12 + (h + 1))
                            if h >= 2:
                                act.wait_ge(s_O, it * 12 + (h - 1))
                            w = LAT if nk == NB else P
                            nc_.activation(probT[:, h % 2, 0:w], ps[:, 2048:2048 + w], ACT.Copy).then_inc(s_pta, 1)

                        exps(0)
                        exps(1)
                        for h in range(12):
                            turned(h)
                            if h < 10:
                                exps(h + 2)
                act.wait_ge(s_on, 1 + 12 * (l * NB + (NB if l == 0 else NBL)))
                act.wait_ge(s_shift, l + 1)
                nc_.activation(zv[0:64, R_WA, :], zv[0:64, R_WA, :], ACT.Tanh)
                nc_.activation(zv[:, R_GL, :], zv[:, R_GL, :], ACT.Sigmoid)
                nc_.activation(zv[0:32, R_MISC, :], zv[0:32, R_MISC, :], ACT.Sigmoid).then_inc(s_gate, 1)
                for n in range(4):
                    act.wait_ge(s_kk, 4 * l + n + 1)
                    nc_.activation(rn[:, n, :], nkk[:, n, :], ACT.Square).then_inc(s_kkq, 1)
                for n in range(12):
                    if n == 2:
                        act.wait_ge(s_kks, l + 1)
                        nc_.activation(small[:, 0:48], ps[:, KS:KS + 48], ACT.Sqrt).then_inc(s_kkr, 1)
                    act.wait_ge(s_rp, 12 * l + n + 1)
                    o = (n % 2) * 1024
                    if n < 2:
                        ins = nc_.activation(vtok[:, :, n * P:(n + 1) * P],
                                             ps[:, o:o + TOK].rearrange("p (b f) -> p b f", b=NB), ACT.Copy)
                    elif n < 6:
                        ins = nc_.activation(aa[:, n - 2, :], ps[:, o:o + TOK], ACT.Sigmoid, bias=par(l, "a0", n - 2))
                    elif n < 10:
                        ins = nc_.activation(sg[:, n - 6, :], ps[:, o:o + TOK], ACT.Sigmoid, bias=par(l, "w0", n - 6))
                    elif n == 10:
                        ins = nc_.activation(gtok[:, 0:4, :], ps[:, o:o + 1024].rearrange("p (b f) -> p b f", b=4), ACT.Copy)
                    else:
                        ins = nc_.activation(gtok[:, 4:6, :], ps[:, o:o + 512].rearrange("p (b f) -> p b f", b=2), ACT.Copy)
                    ins.then_inc(s_rpe, 1)
                act.wait_ge(s_bonin, 2 * (l + 1))
                for f in range(2):
                    ins = nc_.activation(bonus_in[:, f, :], bonus_in[:, f, :], ACT.Identity, scale=par(l, "r_k", f))
                ins.then_inc(s_gate, 1)
                act.wait_ge(s_bonps, l + 1)
                nc_.activation(bon[:, :], ps[:, BONUS:BONUS + NB * 4], ACT.Copy).then_inc(s_bon, 1)
                act.wait_ge(s_prep, 5 * l + 5)
                step0 = NB * l
                for n, b0 in SCAN:
                    with act.Fori(0, n) as i:
                        it = i + step0
                        for g in range(2):
                            r = G[g]
                            off = i * P + b0 * P if g == 0 else i * (-P) + (b0 + n - 1) * P
                            act.wait_ge(s_Sn[g], 1 + it * 2)
                            act.wait_ge(s_AR[g], 1 + it)
                            act.wait_ge(s_BK[g], 1 + it)
                            lo = 1 if g == 0 else 0
                            for f in range(2):
                                nc_.activation(r["ep"][:, f, :, lo:lo + 64],
                                               cs[:, 2 * g + f, ds(off, P)].rearrange("p (c t) -> p c t", c=2),
                                               ACT.Exp, scale=-DECAY)
                            nc_.activation(r["ei"], cs[:, 2 * g:2 * g + 2, ds(off, P)], ACT.Exp,
                                           scale=DECAY).then_inc(s_E[g], 1)
                        for g in range(2):
                            r = G[g]
                            act.wait_ge(s_pre[g], it * 4 + 3)
                            nc_.activation(r["tok"], ps[:, g * 2048:g * 2048 + 1024], ACT.Copy).then_inc(s_tok[g], 1)
                        for j in range(1, len(LEVELS)):
                            for g in range(2):
                                act.wait_ge(s_Tt[g], it * 4 + j)
                                nc_.activation(G[g]["tt"], ps[:, g * 2048 + 512:g * 2048 + 1024].rearrange(
                                    "p (h t) -> p h t", h=4), ACT.Copy).then_inc(s_Tte[g], 1)
                        for g in range(2):
                            r = G[g]
                            act.wait_ge(s_kv[g], 1 + it * 2 + 1)
                            o = g * 2048 + 1536
                            for half in range(2):
                                ins = nc_.activation(r["akv"][:, half::2, :], own_half(o, half), ACT.Copy)
                            ins.then_inc(s_kve[g], 1)
                        for g in range(2):
                            r = G[g]
                            act.wait_ge(s_W[g], it + 1)
                            nc_.activation(r["wt"], ps[:, g * 2048 + 1024:g * 2048 + 1536].rearrange("p (h t) -> p h t", h=4),
                                           ACT.Copy).then_inc(s_Wt[g], 1)
                            act.wait_ge(s_kv[g], 1 + it * 2 + 2)
                            o = g * 2048
                            for half in range(2):
                                ins = nc_.activation(r["uv"][:, half::2, :], own_half(o, half), ACT.Copy)
                            ins.then_inc(s_kve[g], 1)
                        for g in range(2):
                            act.wait_ge(s_y[g], 1 + it + 1)
                            bof = i + b0 if g == 0 else i * (-1) + (b0 + n - 1)
                            for c in range(2):
                                slot = c if g == 0 else 1 - c
                                if g == 0:
                                    dst = hT[64 * c:64 * c + 64, ds(bof * 1024 + 512, 256)]
                                else:
                                    dst = zT[64 * c:64 * c + 64, ds(bof * 256 + R_K * TOK, 256)]
                                src = ps[64 * c:64 * c + 64, g * 2048 + 1024:g * 2048 + 1536].rearrange(
                                    "p (h s i) -> p h s i", h=4, s=2)[:, :, slot, :]
                                ins = nc_.activation(dst.rearrange("p (h i) -> p h i", h=4), src, ACT.Copy)
                            ins.then_inc(s_ye[g], 1)
                    step0 = step0 + n
                nbk = NB if l < DEPTH - 1 else NBL
                act.wait_ge(s_rout, 2 * l + 1)
                nc_.activation(small[:, 48:48 + 4 * nbk], small[:, 48:48 + 4 * nbk], ACT.Sqrt).then_inc(s_rt, 1)
                for f in range(KT):
                    act.wait_ge(s_ot, KT * l + f + 1)
                    t = nbk * P
                    nc_.activation(o_hi[:, f, 0:t], ps[:, (f % 2) * 1024:(f % 2) * 1024 + t], ACT.Copy).then_inc(s_ote, 1)
                t = TOK if l < DEPTH - 1 else LAT
                with act.Fori(0, KT // SLOTS) as i:
                    for q in range(SLOTS):
                        act.wait_ge(s_tile[q], 1 + i + (TILES * l + T_OUT + 1))
                        src = ps[:, (q % 2) * 1024:(q % 2) * 1024 + t]
                        nc_.activation(zT[:, ds(i * (SLOTS * TOK) + q * TOK, t)], src, ACT.Copy)
                        nc_.activation(zT[:, ds(i * (SLOTS * TOK) + (KT + q) * TOK, t)], src, ACT.Square).then_inc(s_ev, 1)
                root(4 * l + 1, nbk)
                squares(l, 2, xv)
                root(4 * l + 2, nbk)
                first_parts(l, 2)
                with act.Fori(0, FFG) as i:
                    for n in range(2, 2 * KT):
                        q = n % SLOTS
                        act.wait_ge(s_slab[q], i * 64 + 16 * (FILLS * l + F_MLP + n // SLOTS + 1))
                        k = n - 2
                        act.wait_ge(s_tile[k % SLOTS], 1 + i * 4 + (TILES * l + T_MLP + k // SLOTS + 1))
                        nc_.activation(whi[q % 2], slab[:, q * SLAB:(q + 1) * SLAB], ACT.Copy).then_inc(s_whi, 1)
                        if k < KT:
                            act.wait_ge(s_h1, 1 + i * KT + (32 * l + (k - 1 if k >= 2 else 0)))
                            nc_.activation(h1[:, k % 2, 0:t], ps[:, (k % 2) * 1024:(k % 2) * 1024 + t],
                                           ACT.Relu).then_inc(s_ev, 1)
                squares(l, 3, yT)
                root(4 * l + 3, nbk)

        @block.vector
        def _(dve):
            ch = Chain(dve, s_dve)
            V = nc.vector

            def pars(l, name, n, k=0):
                return pcol[:, l * NPC + PC[name] + k:l * NPC + PC[name] + k + n]

            V.memset(eps[:, :], EPS).then_inc(s_eps, 1)
            dve.wait_ge(s_silu, 1)
            V.tensor_tensor(silu[:, :], silu[:, :], cT[:, :], ALU.mult).then_inc(s_silu, 1)

            def gn_roots(n):
                return n // 4 + (1 if n % 4 else 0)

            def add_square(l, which, k, t):
                if which == 1:
                    dve.wait_ge(s_ev, 1 + 60 * l + NZ + k + 1)
                else:
                    dve.wait_ge(s_sq, SQ * l + k + 1)
                ins = V.tensor_tensor(sq[:, 0, 0:t], sq[:, 0, 0:t], sq[:, k, 0:t], ALU.add)
                if k < KT - 1:
                    ch.link(ins)
                else:
                    ins.then_inc(s_acc, 1)

            def squares(l):
                for k in range(KT):
                    V.tensor_tensor(sq[:, k, :], xv[:, k, :], xv[:, k, :], ALU.mult).then_inc(s_sq, 1)
                for k in range(1, KT):
                    add_square(l, 0, k, TOK)

            def inverse_root(n, t):
                dve.wait_ge(s_rt, n + 1 + gn_roots(n))
                V.reciprocal(rcol[:, 0:t // P], rcol[:, 0:t // P]).then_inc(s_rec, 1)
                dve.wait_ge(s_rs, n + 1)

            def before_mixer(l):
                for k in range(KT + 1):
                    if k < KT:
                        for s, a, b in segs(l, False):
                            ins = V.tensor_scalar(hv[:, k, a:b], hv[:, k, a:b], gv[:, 0, k, s:s + 1], mv[:, k, s:s + 1],
                                                  ALU.mult, ALU.add)
                        ins.then_inc(s_xn, 1)
                    if k:
                        dve.wait_ge(s_h, 16 * l + k)
                        V.tensor_tensor(pre_lo[:, k - 1, :], hv[:, k - 1, :], pre_hi[0][:, k - 1, :],
                                        ALU.subtract).then_inc(s_hlo, 1)

            def before_mlp(l):
                inverse_root(4 * l + 2, TOK if l < DEPTH - 1 else LAT)
                for k in range(KT + 1):
                    if k < KT:
                        for s, a, b in segs(l, True):
                            ins = V.scalar_tensor_tensor(out=hv[:, k, a:b], in0=xv[:, k, a:b], scalar=gv[:, 2, k, s:s + 1],
                                                         in1=rs[:, a:b], op0=ALU.mult, op1=ALU.mult)
                        ins.then_inc(s_xn, 1)
                    if k:
                        dve.wait_ge(s_h, 16 * l + 8 + k)
                        for s, a, b in segs(l, True):
                            ins = V.scalar_tensor_tensor(out=pre_lo[:, k - 1, a:b], in0=hv[:, k - 1, a:b],
                                                         scalar=mv[:, 23 + k, s:s + 1], in1=pre_hi[2][:, k - 1, a:b],
                                                         op0=ALU.add, op1=ALU.subtract)
                        ins.then_inc(s_hlo, 1)

            def post(l, which):
                t = TOK if l < DEPTH - 1 else LAT
                inverse_root(4 * l + which, t)
                for k in range(KT):
                    ch.link(V.tensor_tensor(yT[:, k, 0:t], yT[:, k, 0:t], rs[:, 0:t], ALU.mult))
                    for s, a, b in segs(l, True):
                        ins = V.scalar_tensor_tensor(out=xv[:, k, a:b], in0=yT[:, k, a:b],
                                                     scalar=gv[:, which, k, s:s + 1],
                                                     in1=xv[:, k, a:b], op0=ALU.mult, op1=ALU.add)
                    ins.then_inc(s_xup, 1)

            for l in range(DEPTH):
                if l == 0:
                    dve.wait_ge(s_x, 16 * KT)
                else:
                    dve.wait_ge(s_xup, 16 * l)
                squares(l)
                inverse_root(4 * l, TOK)
                for k in range(KT):
                    ins = V.tensor_tensor(hv[:, k, :], xv[:, k, :], rs, ALU.mult)
                ch.link(ins)
                if l == 0:
                    dve.wait_ge(s_maskraw, 16)
                    V.tensor_copy(km[:, :], zT[:, 0:NKM * P]).then_inc(s_masks, 1)
                dve.wait_ge(s_modps, l + 1)
                if l:
                    dve.wait_ge(s_h, 16)
                ch.link(V.tensor_tensor(mv, ps[:, 3584:3584 + 2 * NMOD].rearrange("p (k s) -> p k s", s=2),
                                        pars(l, "b_mod", NMOD).unsqueeze(2).to_broadcast([P, NMOD, 2]), ALU.add))
                for n, (name, part, plus) in enumerate((("g_pre_mix", 8, 1), ("g_post_mix", 16, 0),
                                                        ("g_pre_mlp", 32, 1), ("g_post_mlp", 40, 0))):
                    if plus:
                        ch.link(V.tensor_scalar(gv[:, n], mv[:, part:part + 8, :], 1.0, None, ALU.add))
                    V.tensor_tensor(gv[:, n], gv[:, n] if plus else mv[:, part:part + 8, :],
                                    pars(l, name, 8).unsqueeze(2).to_broadcast([P, 8, 2]), ALU.mult)
                V.tensor_scalar(omm[:, 0:9], pars(l, "mu", 9), -1.0, 1.0, ALU.mult, ALU.add)
                V.tensor_scalar(omm[:, 9:18], pars(l, "mu", 9), 0.5, None, ALU.mult)
                V.tensor_scalar(omm[:, 18:22], pars(l, "k_a", 4), -1.0, 1.0, ALU.mult, ALU.add)
                ch.link(V.tensor_scalar(omm[:, 22:26], pars(l, "sink", 4), -1.0, None, ALU.mult))
                dve.sem_inc(s_modT, 1)
                before_mixer(l)

                for n, (tile, name) in enumerate(((A_Q, "q_norm"), (A_Q + 1, "q_norm"), (A_K, "k_norm"),
                                                  (C_Q, "cq_norm"), (C_KV, "ckv_norm"))):
                    if n == 0:
                        dve.wait_ge(s_prt, l + 1)
                        V.reciprocal(small[:, 0:48], small[:, 0:48]).then_inc(s_prec, 1)
                    dve.wait_ge(s_psp, 5 * l + n + 1)
                    r = ps[:, ASPREAD[n]:ASPREAD[n] + TOK]
                    for j in range(2 if tile == C_Q else 1):
                        V.scalar_tensor_tensor(out=zv[:, tile + j, :], in0=zv[:, tile + j, :], scalar=pars(l, name, 1, j),
                                               in1=r, op0=ALU.mult, op1=ALU.mult).then_inc(s_pn, 1)
                dve.wait_ge(s_atab, 64 * (l + 1))
                for n, (where, tile) in enumerate(ROPES):
                    if n == 7:
                        dve.wait_ge(s_paire, 12 * l + 6)
                        for q in (qa, qd):
                            for g in range(2):
                                ins = V.memset(q[64 - 64 * g:128 - 64 * g, 2 * g:2 * g + 2, :], 0.0)
                        ins.then_inc(s_qz, 1)
                    p = 96 if where != 64 else P
                    tab = 2 if where != 64 else 0
                    x = qB[0:p, tile, 0:LAT] if where == "q" else zv[0:p, tile, 0:LAT]
                    dst = zv[:, D_V, P:P + LAT] if tile == D_K and where == 64 else x
                    o = 1024 + (n % 4) * 512
                    tmp = work[0:p, W_PT + (n % 2) * LAT:W_PT + (n % 2) * LAT + LAT]
                    dve.wait_ge(s_rot, 11 * l + n + 1)
                    V.tensor_tensor(tmp, ps[0:p, o:o + LAT], rope[0:p, tab + 1, :], ALU.mult)
                    ch.link(V.tensor_tensor(x, x, rope[0:p, tab, :], ALU.mult))
                    if tile == D_K and where == 64:
                        dve.wait_ge(s_pair, 12 * l + 2)
                    V.tensor_tensor(dst, x, tmp, ALU.add).then_inc(s_roped, 1)

                dve.wait_ge(s_paire, 12 * (l + 1))
                for n, b0 in streams(l):
                    nk = NB if b0 == 0 else NBC
                    win = b0 == 0
                    with dve.Fori(0, n) as i:
                        it = i + (l * NB + b0)
                        ch.enter(i, (8 if win else 4) + 12 + 4)

                        def peak(h):
                            dve.wait_ge(s_S, 1 + it * 12 + (h + 1))
                            o = (h % 2) * 1024
                            src = ps[:, o:o + nk * P]
                            if h >= 8 and win:
                                dve.wait_ge(s_T, it * 12 + (h - 1))
                                V.tensor_tensor(prob[:, h % 2, 0:384], ps[:, o:o + 384],
                                                work[:, ds(i * 384 + W_WMASK, 384)], ALU.add)
                                ch.link(V.tensor_copy(prob[:, h % 2, 384:640], ps[:, o + 512:o + TOK]))
                                src = prob[:, h % 2, 0:640]
                            nm = small[:, h:h + 1]
                            ins = V.tensor_reduce(nm, src, AX.X, ALU.max, negate=True)
                            if h >= 8:
                                ch.link(ins)
                                V.tensor_tensor(nm, nm, omm[:, 22 + h - 8:23 + h - 8], ALU.min).then_inc(s_nm, 1)
                            else:
                                ins.then_inc(s_nm, 1)

                        def turned(h):
                            dve.wait_ge(s_T, it * 12 + (h + 1))
                            if h >= 2:
                                dve.wait_ge(s_O, it * 12 + (h - 1))
                            a = LAT if win else P
                            n_ = P if h >= 8 or not win else CTX
                            V.tensor_copy(probT[:, h % 2, a:a + n_], ps[:, 2560:2560 + n_]).then_inc(s_ptd, 1)

                        def normed(h):
                            sm = small[:, 16 + h:17 + h]
                            dve.wait_ge(s_P, 1 + it * 12 + (h + 1))
                            if h >= 8:
                                dve.wait_ge(s_es, it * 4 + (h - 7))
                                ch.link(V.tensor_tensor(sm, sm, small[:, 32 + h:33 + h], ALU.add))
                            ch.link(V.reciprocal(sm, sm))
                            dve.wait_ge(s_O, it * 12 + (h + 1))
                            grp, hh = h // 4, h % 4
                            col = (0, 256, 768)[grp] + hh * 64
                            half = (hh % 2) if grp == 1 else hh // 2
                            o = 3072 + (h % 2) * 512 + half * 64
                            V.tensor_scalar(hT[:, ds(i * 1024 + (b0 * 1024 + col), 64)], ps[:, o:o + 64], sm, None,
                                            ALU.mult).then_inc(s_on, 1)

                        peak(0)
                        peak(1)
                        for h in range(12):
                            turned(h)
                            if h < 10:
                                peak(h + 2)
                            normed(h)
                        ch.leave(n)

                dve.wait_ge(s_shift, l + 1)
                for n in range(4):
                    V.tensor_scalar(nkk[:, n, :], zv[:, R_K + n % 2, :], pars(l, "k_k", 1, n), None,
                                    ALU.mult).then_inc(s_kk, 1)
                dve.wait_ge(s_kkr, l + 1)
                ch.link(V.tensor_scalar(small[:, 0:48], small[:, 0:48], 1e-12, None, ALU.max))
                V.reciprocal(small[:, 0:48], small[:, 0:48]).then_inc(s_krec, 1)
                for n in range(4):
                    dve.wait_ge(s_ksp, 4 * l + n + 1)
                    o = 2048 + (n % 2) * 1024
                    V.scalar_tensor_tensor(out=nkk[:, n, :], in0=nkk[:, n, :], scalar=-1.0, in1=ps[:, o:o + TOK],
                                           op0=ALU.mult, op1=ALU.mult).then_inc(s_kkn, 1)
                dve.wait_ge(s_kkn, 4 * (l + 1))
                for n in range(4):
                    dve.wait_ge(s_rpe, 12 * l + n + 3)
                    ch.link(V.scalar_tensor_tensor(out=bh[:, n, :], in0=nkk[:, n, :], scalar=-1.0, in1=aa[:, n, :],
                                                   op0=ALU.mult, op1=ALU.mult))
                    ch.link(V.tensor_scalar(aa[:, n, :], aa[:, n, :], pars(l, "k_a", 1, n), omm[:, 18 + n:19 + n],
                                            ALU.mult, ALU.add))
                    V.tensor_tensor(kd[:, n, :], aa[:, n, :], zv[:, R_K + n % 2, :], ALU.mult).then_inc(s_prep, 1)
                dve.wait_ge(s_rtab, 64 * (l + 1))
                for n in range(4):
                    dve.wait_ge(s_rpe, 12 * l + 7 + n)
                    if n == 2:
                        dve.wait_ge(s_rp, 12 * l + 10)
                    if n == 3:
                        dve.wait_ge(s_rp, 12 * (l + 1))
                    ch.link(V.tensor_tensor_scan(cs[:, n, :], smask, sg[:, n, :], 0.0, ALU.mult, ALU.add))
                    if n >= 2:
                        ch.link(V.tensor_tensor(sg[:, n, :], sg[:, n, :], cs[:, n, :], ALU.subtract))
                        c3 = cs[:, n, :].rearrange("p (c t) -> p c t", t=CH)
                        s3 = sg[:, n, :].rearrange("p (c t) -> p c t", t=CH)
                        ch.link(V.tensor_tensor(s3, s3, c3[:, :, CH - 1:CH].to_broadcast([P, TOK // CH, CH]), ALU.add))
                        ch.link(V.tensor_copy(cs[:, n, :], sg[:, n, :]))
                dve.wait_ge(s_rpe, 12 * (l + 1))
                for g in range(2):
                    lo = 0 if g == 0 else 64
                    V.memset(G[g]["ep"][:, :, :, lo:lo + 1], 1.0)
                    for h, f, rows in HEADS:
                        V.memset(G[g]["ar"][64 - rows.start:128 - rows.start, h, :, :], 0.0)
                    ch.link(V.memset(st[g], 0.0))
                dve.sem_inc(s_prep, 1)

                step0 = NB * l
                for n, b0 in SCAN:
                    with dve.Fori(0, n) as i:
                        it = i + step0
                        ch.enter(i, 2 * (1 + 2))
                        for g in range(2):
                            r = G[g]
                            off = i * P + b0 * P if g == 0 else i * (-P) + (b0 + n - 1) * P
                            lo = (0, 1) if g == 0 else (1, 0)
                            dve.wait_ge(s_E[g], it + 1)
                            dve.wait_ge(s_y[g], 1 + it)
                            for h, f, rows in HEADS:
                                for j, src in enumerate((nkk[rows, 2 * g + f, ds(off, P)], zv[rows, R_R + f, ds(off, P)])):
                                    ins = V.tensor_tensor(r["ar"][rows, h, j, :].rearrange("p (c t) -> p c t", c=2),
                                                          src.rearrange("p (c t) -> p c t", c=2),
                                                          r["ep"][rows, f, :, lo[j]:lo[j] + 64], ALU.mult)
                            ins.then_inc(s_AR[g], 1)
                        for g in range(2):
                            r = G[g]
                            m2 = mask(g, 0, 2).unsqueeze(1).to_broadcast([P, 4, 256])
                            dve.wait_ge(s_pre[g], it * 4 + 1)
                            V.tensor_tensor(r["abr"], ps[:, g * 2048:g * 2048 + 1024].rearrange("p (h t) -> p h t", h=4),
                                            m2, ALU.mult).then_inc(s_msk[g], 1)
                            dve.wait_ge(s_pre[g], it * 4 + 2)
                            V.tensor_tensor(r["akr"], ps[:, g * 2048 + 1024:g * 2048 + 2048].rearrange(
                                "p (h t) -> p h t", h=4), m2, ALU.mult).then_inc(s_msk[g], 1)
                        for g in range(2):
                            r = G[g]
                            dve.wait_ge(s_pre[g], it * 4 + 4)
                            ch.link(V.tensor_tensor(r["t"], ps[:, g * 2048 + 1024:g * 2048 + 1536].rearrange(
                                "p (h t) -> p h t", h=4), mask(g, 2).unsqueeze(1).to_broadcast([P, 4, P]), ALU.mult))
                            V.tensor_tensor(r["t"], r["t"], ident.unsqueeze(1).to_broadcast([P, 4, P]),
                                            ALU.add).then_inc(s_msk[g], 1)
                        for j in range(len(LEVELS)):
                            for g in range(2):
                                dve.wait_ge(s_X[g], it * 5 + (j + 1))
                                V.tensor_tensor(G[g]["x"], ps[:, g * 2048 + 1536:g * 2048 + 2048].rearrange(
                                    "p (h t) -> p h t", h=4), mask(g, 4 + j).unsqueeze(1).to_broadcast([P, 4, P]),
                                    ALU.mult).then_inc(s_Xm[g], 1)
                            for g in range(2):
                                r = G[g]
                                dve.wait_ge(s_Tp[g], it * 5 + (j + 1))
                                x, o = (r["t"], g * 2048) if j < len(LEVELS) - 1 else (r["tt"], g * 2048 + 512)
                                V.tensor_tensor(x, x, ps[:, o:o + 512].rearrange("p (h t) -> p h t", h=4),
                                                ALU.add).then_inc(s_Tu[g], 1)
                        for k in range(2):
                            for g in range(2):
                                r = G[g]
                                c = k if g == 0 else 1 - k
                                rows = slice(64 * c, 64 * c + 64)
                                dve.wait_ge(s_U[g], it * 2 + (k + 1))
                                if k == 0:
                                    dve.wait_ge(s_kve[g], it * 2 + 2)
                                V.tensor_tensor(r["u"][rows], ps[rows, g * 2048 + 512:g * 2048 + 1024].rearrange(
                                    "p (h s i) -> p h s i", h=4, s=2)[:, :, k, :], r["uv"][rows],
                                    ALU.add).then_inc(s_Us[g], 1)
                            for g in range(2):
                                r = G[g]
                                c = k if g == 0 else 1 - k
                                end = 64 if g == 0 else 0
                                dve.wait_ge(s_dS[g], it * 2 + (k + 1))
                                ch.link(V.tensor_tensor(s1[g], st[g][:, :, k, :], ps[:, g * 2048 + 1536:g * 2048 + 1664]
                                                        .rearrange("p (f i) -> p f i", f=2), ALU.add))
                                if k == 1:
                                    dve.wait_ge(s_y[g], 1 + it + 1)
                                V.tensor_tensor(st[g][:, :, 1 - k, :], s1[g],
                                                r["ep"][:, :, c, end:end + 1].to_broadcast([P, 2, 64]),
                                                ALU.mult).then_inc(s_Sn[g], 1)
                        ch.leave(n)
                    step0 = step0 + n

                nbk = NB if l < DEPTH - 1 else NBL
                for g in range(2):
                    dve.wait_ge(s_ye[g], 1 + NB * (l + 1))
                y = yrev[:, 0:nbk, :]
                y4 = yrev[:, 0:nbk, :].rearrange("p b (h i) -> p b h i", h=4)
                vt = vtok[:, 0:nbk, :]
                v4 = vt.rearrange("p b (h i) -> p b h i", h=4)
                tmp = wv(W_SCR, NB, 256)[:, 0:nbk, :]
                t4 = tmp.rearrange("p b (h i) -> p b h i", h=4)
                mean = small[:, 72:72 + 4 * nbk]
                var = small[:, 48:48 + 4 * nbk]
                b4 = [P, nbk, 4, 64]
                ch.link(V.tensor_tensor(y, y, mix[:, 0:nbk, 512:768], ALU.add))
                ch.link(V.tensor_reduce(mean, y4, AX.X, ALU.add))
                ch.link(V.tensor_scalar(mean, mean, 1.0 / 64, None, ALU.mult))
                ch.link(V.tensor_tensor(y4, y4, mean.rearrange("p (b h) -> p b h", h=4).unsqueeze(3).to_broadcast(b4),
                                        ALU.subtract))
                ch.link(V.tensor_tensor(tmp, y, y, ALU.mult))
                ch.link(V.tensor_reduce(var, t4, AX.X, ALU.add))
                V.tensor_scalar(var, var, 1.0 / 64, GN_EPS, ALU.mult, ALU.add).then_inc(s_rout, 1)
                dve.wait_ge(s_bon, l + 1)
                ch.link(V.tensor_tensor(v4, v4, bon[:, 0:4 * nbk].rearrange("p (b h) -> p b h", h=4).unsqueeze(3)
                                        .to_broadcast(b4), ALU.mult))
                dve.wait_ge(s_rt, 5 * l + 2)
                ch.link(V.reciprocal(var, var))
                ch.link(V.tensor_tensor(y4, y4, var.rearrange("p (b h) -> p b h", h=4).unsqueeze(3).to_broadcast(b4),
                                        ALU.mult))
                dve.wait_ge(s_ln, 32 * (l + 1))
                ch.link(V.tensor_tensor(y, y, lnw.unsqueeze(1).to_broadcast([P, nbk, 256]), ALU.mult))
                ch.link(V.tensor_tensor(y, y, lnb.unsqueeze(1).to_broadcast([P, nbk, 256]), ALU.add))
                ch.link(V.tensor_tensor(y, y, vt, ALU.add))
                V.tensor_tensor(mix[:, 0:nbk, 512:768], y, gtok[:, 0:nbk, :], ALU.mult).then_inc(s_rout, 1)

                t = TOK if l < DEPTH - 1 else LAT
                for f in range(KT):
                    dve.wait_ge(s_ote, KT * l + f + 1)
                    V.tensor_tensor(o_lo[:, f, 0:t], ps[:, (f % 2) * 1024:(f % 2) * 1024 + t], o_hi[:, f, 0:t],
                                    ALU.subtract).then_inc(s_otl, 1)

                for k in range(1, KT):
                    add_square(l, 1, k, t)
                post(l, 1)
                before_mlp(l)
                for k in range(KT):
                    ins = V.memset(yT[:, k, 0:t], 0.0)
                ch.link(ins)
                with dve.Fori(0, FFG) as i:
                    ch.enter(i, 2 * KT)
                    for k in range(KT):
                        dve.wait_ge(s_ev, 1 + i * KT + (60 * l + NZ + KT + k + 1))
                        raw = h1[:, k % 2, 0:t]
                        ch.link(V.tensor_tensor(raw, raw, raw, ALU.mult))
                        ch.link(V.tensor_copy(h1_hi[:, k, 0:t], raw))
                        V.tensor_tensor(h1_lo[:, k, 0:t], raw, h1_hi[:, k, 0:t], ALU.subtract).then_inc(s_h1, 1)
                    dve.wait_ge(s_ev2, 1 + i * KT + 32 * l)
                    for k in range(KT):
                        dve.wait_ge(s_tile[k % SLOTS], 1 + i * 4 + (TILES * l + T_MLP + 2 + k // SLOTS + 1))
                        o = 2048 + (k % 2) * 1024
                        V.tensor_tensor(yT[:, k, 0:t], yT[:, k, 0:t], ps[:, o:o + t], ALU.add).then_inc(s_ev2, 1)
                    ch.leave(FFG)
                dve.wait_ge(s_ev2, 1 + 32 * (l + 1))
                post(l, 3)

        @block.tensor
        def _(pe):
            def mm(out, lhsT, rhs, start=True, stop=True):
                return pe.matmul(out, lhsT, rhs, start=start, stop=stop)

            fills = [0]

            def product(hi, lo, o, q, fill, t, ready=None):
                pe.wait_ge(s_used[q], fill + 2)
                for a, b in ((0, LAT), (LAT, TOK)) if t == TOK else ((0, LAT),):
                    out = ps[:, o + a:o + b]
                    for k in range(KT):
                        if ready is not None and a == 0:
                            pe.wait_ge(ready[0], ready[1] + k)
                        w1, w2 = (w[q % 2][:, k * P:(k + 1) * P] for w in (whi, wlo))
                        mm(out, w1, hi[:, k, a:b], k == 0, False)
                        mm(out, w1, lo[:, k, a:b], False, False)
                        ins = mm(out, w2, hi[:, k, a:b], False, k == KT - 1)
                return ins

            def ssq(l, which):
                n = 4 * l + which
                nb = NB if which == 0 or l < DEPTH - 1 else NBL
                pe.wait_ge(s_acc, n + 1)
                for b in range(nb):
                    ins = mm(ps[:, NS + b:NS + b + 1], sq[:, 0, b * P:(b + 1) * P], ones[:, 0:1])
                ins.then_inc(s_ssq, 1)
                pe.wait_ge(s_rec, n + 1)
                for b in range(nb):
                    ins = mm(ps[:, RS + b * P:RS + (b + 1) * P], rcol[:, b:b + 1].to_broadcast([P, P]), ident)
                ins.then_inc(s_rs, 1)

            def keep_clock(o, n):
                for _ in range(n):
                    mm(ps[:, o:o + 512], ident, kf[:, 0:512])

            def spread_heads(o, col):
                for j in range(2):
                    ins = mm(ps[64 * j:64 * j + 64, o:o + P], small[:, col + j:col + j + 1].to_broadcast([P, 64]), ident)
                return ins

            pe.wait_ge(s_silu, 2)
            pe.wait_ge(s_const, 48)
            for l in range(DEPTH):
                t = TOK if l < DEPTH - 1 else LAT
                nbk = t // P
                def modulation(first):
                    with pe.Fori(0, 6) as i:
                        pe.wait_ge(s_modrow, 1 + i + (12 * l + first))
                        for q in range(SLOTS):
                            pe.wait_ge(s_slab[q], i * 16 + 16 * (fills[0] + 1))
                            for j in range(2):
                                k = 2 * q + j
                                ins = mm(ps[0:2, 3584:4096], silu[:, 2 * k:2 * k + 2],
                                         slab[:, q * SLAB + j * 512:q * SLAB + (j + 1) * 512], k == 0, k == KT - 1)
                            ins.then_inc(s_used[q], 1)
                    fills[0] += 6

                modulation(0)
                ssq(l, 0)
                modulation(6)
                pe.wait_ge(s_modrow, 1 + 12 * (l + 1))
                for m in range(NMOD):
                    ins = pe.transpose(ps[:, 3584 + 2 * m:3586 + 2 * m], work[0:2, m * P:(m + 1) * P], ident[0:2, 0:2])
                ins.then_inc(s_modps, 1)
                keep_clock(0, 11)
                with pe.Fori(0, NZ // SLOTS) as i:
                    for q in range(SLOTS):
                        tile = i * SLOTS + (60 * l + q)
                        if l or q >= 2:
                            pe.wait_ge(s_ev, 1 + tile - 1)
                        else:
                            pe.wait_ge(s_ev, 1 + i * SLOTS)
                        ins = product(pre_hi[0], pre_lo, (q % 2) * 1024, q, i + fills[0], TOK,
                                      (s_hlo, 16 * l + 1) if q == 0 else None)
                        ins.then_inc(s_tile[q], 1)
                fills[0] += NZ // SLOTS
                pe.wait_ge(s_ev, 1 + 60 * l + NZ)

                def turn(n, tile):
                    o = (n % 2) * 3072
                    for b in range(NB):
                        ins = pe.transpose(ps[:, o + b * P:o + (b + 1) * P], zv[:, tile, b * P:(b + 1) * P], ident)
                    ins.then_inc(s_pair, 1)

                def latent(n):
                    pe.wait_ge(s_paire, 12 * l + n - 1)
                    o = (n % 2) * 3072
                    if n < 10:
                        for a, b in ((0, LAT), (LAT, TOK)):
                            if n < 6:
                                for k in range(2):
                                    ins = mm(ps[0:96, o + a:o + b], uq[:, k, (n - 2) * 96:(n - 1) * 96],
                                             zv[:, C_Q + k, a:b], k == 0, k == 1)
                            else:
                                ins = mm(ps[0:64, o + a:o + b], ukv[:, (n - 6) * P:(n - 6) * P + 64], zv[:, C_KV, a:b])
                    else:
                        vcols = ukv.rearrange("p (h c) -> p h c", h=4)[:, :, 64:128]
                        for b in (range(4) if n == 10 else range(4, 6)):
                            ins = mm(ps[:, o + (b % 4) * 256:o + (b % 4) * 256 + 256], zv[:, C_KV, b * P:(b + 1) * P], vcols)
                    ins.then_inc(s_pair, 1)

                def rotate(n):
                    where, tile = ROPES[n]
                    o = 1024 + (n % 4) * 512
                    if n >= 4:
                        pe.wait_ge(s_roped, 11 * l + n - 3)
                    if where == 64:
                        ins = mm(ps[:, o:o + LAT], rot64, zv[:, tile, 0:LAT])
                    else:
                        x = qB[0:96, tile, 0:LAT] if where == "q" else zv[0:96, tile, 0:LAT]
                        ins = mm(ps[0:96, o:o + LAT], rot96, x)
                    ins.then_inc(s_rot, 1)

                turn(0, A_V)
                turn(1, D_V)
                pe.wait_ge(s_psq, 6 * (l + 1))
                for n in range(3):
                    for b in range(NB):
                        mm(ps[:, AS + 12 * n + 2 * b:AS + 12 * n + 2 * b + 2],
                           work[:, n * TOK + b * P:n * TOK + (b + 1) * P], bd[:, 0:P:64])
                for at, tiles in ((36, (3, 4)), (42, (5,))):
                    for b in range(NB):
                        for n in tiles:
                            ins = mm(ps[:, AS + at + b:AS + at + b + 1], work[:, n * TOK + b * P:n * TOK + (b + 1) * P],
                                     ones[:, 0:1], n == tiles[0], n == tiles[-1])
                ins.then_inc(s_pss, 1)
                pe.wait_ge(s_prec, l + 1)
                for n, o in enumerate(ASPREAD):
                    if n == 2:
                        pe.wait_ge(s_paire, 12 * l + 1)
                    if n == 3:
                        pe.wait_ge(s_paire, 12 * l + 2)
                    if n == 4:
                        pe.wait_ge(s_pn, 6 * l + 1)
                    for b in range(NB):
                        if n < 3:
                            ins = spread_heads(o + b * P, 12 * n + 2 * b)
                        else:
                            r = small[:, 18 + 6 * n + b:19 + 6 * n + b].to_broadcast([P, P])
                            ins = mm(ps[:, o + b * P:o + (b + 1) * P], r, ident)
                    ins.then_inc(s_psp, 1)
                pe.wait_ge(s_pn, 6 * (l + 1))
                for n in range(7):
                    rotate(n)
                pe.wait_ge(s_atab, 64 * (l + 1))
                pe.wait_ge(s_pn, 6 * (l + 1))
                for n in range(2, 12):
                    latent(n)
                for n in range(7, 11):
                    rotate(n)
                pe.wait_ge(s_paire, 12 * (l + 1))
                keep_clock(0, 7)
                pe.wait_ge(s_roped, 11 * (l + 1))
                pe.wait_ge(s_krc, l + 1)
                pe.wait_ge(s_pads, 2 * (l + 1))
                pe.wait_ge(s_qz, l + 1)
                for n, b0 in streams(l):
                    win = b0 == 0
                    nk = NB if win else NBC
                    with pe.Fori(0, n) as i:
                        it = i + (l * NB + b0)

                        def scores(h):
                            if h >= 2:
                                pe.wait_ge(s_P, 1 + it * 12 + (h - 1))
                            else:
                                pe.wait_ge(s_P, 1 + it * 12)
                            grp, hh = h // 4, h % 4
                            o = (h % 2) * 1024
                            if h == 4:
                                pe.wait_ge(s_qt, it + 1)
                            if grp == 1:
                                q, k, rows = qb[0:96, hh, :], kB[:, hh, :], slice(0, 96)
                            else:
                                rows = slice(0, P)
                                q = (qa, None, qd)[grp][:, hh, :]
                                k = zv[:, (A_K, None, D_K)[grp], :]
                            if win and grp == 2:
                                if hh == 0:
                                    pe.wait_ge(s_kw, i + (NBL * l + 1))
                                mm(ps[:, o:o + 384], q, kwin[rows, :])
                            elif win:
                                mm(ps[:, o:o + LAT], q, k[rows, 0:LAT])
                            oc = o + LAT if win else o
                            mm(ps[:, oc:oc + CTX], q, k[rows, LAT:TOK]).then_inc(s_S, 1)

                        def turns(h):
                            pe.wait_ge(s_P, 1 + it * 12 + (h + 1))
                            pe.wait_ge(s_pta, 1 + it * 12 + h)
                            pe.wait_ge(s_ptd, 1 + it * 12 + h)
                            for b in range(5 if win and h >= 8 else nk):
                                c = 2048 + b * (P if win else 512)
                                ins = pe.transpose(ps[:, c:c + P],
                                                   prob[:, h % 2, b * P:(b + 1) * P], ident)
                            ins.then_inc(s_T, 1)

                        def output(h):
                            pe.wait_ge(s_pta, 1 + it * 12 + (h + 1))
                            pe.wait_ge(s_ptd, 1 + it * 12 + (h + 1))
                            if h >= 2:
                                pe.wait_ge(s_on, 1 + it * 12 + (h - 1))
                            grp, hh = h // 4, h % 4
                            o = 3072 + (h % 2) * 512
                            kb = list(range(NB)) if win else list(range(NBL, NB))
                            if grp == 2 and win:
                                kb = [0, 1, 2, NBL, NBL + 1]
                            for j, b in enumerate(kb):
                                if grp == 0:
                                    v = vA[:, b, :]
                                elif grp == 1:
                                    v = vB[:, b, (hh // 2) * P:(hh // 2) * P + P]
                                elif win and j < 3:
                                    v = work[:, ds(i * P + (W_VD + j * P), P)]
                                else:
                                    v = vD[:, b + 2, :]
                                ins = mm(ps[:, o:o + P], probT[:, h % 2, j * P:(j + 1) * P], v, j == 0, j == len(kb) - 1)
                            ins.then_inc(s_O, 1)

                        pe.wait_ge(s_qa, it + 1)
                        pe.wait_ge(s_on, 1 + it * 12)
                        scores(0)
                        scores(1)
                        for h in range(12):
                            turns(h)
                            if h < 10:
                                scores(h + 2)
                            output(h)

                pe.wait_ge(s_on, 1 + (12 * (l * NB + (NB if l == 0 else NBL))))
                pe.wait_ge(s_shift, l + 1)
                for n in range(12):
                    if n >= 2:
                        pe.wait_ge(s_rpe, 12 * l + n - 1)
                    o = (n % 2) * 1024
                    if n < 2:
                        for b in range(NB):
                            ins = pe.transpose(ps[:, o + b * P:o + (b + 1) * P], zv[:, R_V + n, b * P:(b + 1) * P], ident)
                    elif n < 10:
                        if n == 2:
                            pe.wait_ge(s_gate, 2 * l + 1)
                            pe.wait_ge(s_rtab, 64 * (l + 1))
                        c = (512 if n < 6 else 0) + ((n - 2) % 4) * P
                        for a, b in ((0, LAT), (LAT, TOK)):
                            ins = mm(ps[:, o + a:o + b], w2a2[:, c:c + P], zv[:, R_WA, a:b])
                    else:
                        for b in (range(4) if n == 10 else range(4, 6)):
                            c = o + (b % 4) * 256
                            mm(ps[:, c:c + 256], zv[:, R_GL, b * P:(b + 1) * P], g2a, True, False)
                            ins = mm(ps[:, c:c + 256], zv[0:32, R_MISC, b * P:(b + 1) * P], g2b, False, True)
                    ins.then_inc(s_rp, 1)
                    if n == 1:
                        keep_clock(2048, 3)
                        pe.wait_ge(s_kkq, 4 * (l + 1))
                        for m in range(4):
                            for b in range(NB):
                                c = KS + 12 * m + 2 * b
                                ins = mm(ps[:, c:c + 2], rn[:, m, b * P:(b + 1) * P], bd[:, 0:P:64])
                        ins.then_inc(s_kks, 1)
                    if n == 3:
                        pe.wait_ge(s_krec, l + 1)
                        for m in range(4):
                            if m >= 2:
                                pe.wait_ge(s_kkn, 4 * l + m - 1)
                            for b in range(NB):
                                ins = spread_heads(2048 + (m % 2) * 1024 + b * P, 12 * m + 2 * b)
                            ins.then_inc(s_ksp, 1)
                pe.wait_ge(s_kkn, 4 * (l + 1))
                keep_clock(2048, 6)
                pe.wait_ge(s_gate, 2 * l + 2)
                for b in range(NB):
                    for f in range(2):
                        ins = mm(ps[:, BONUS + b * 4 + 2 * f:BONUS + 2 + b * 4 + 2 * f], bonus_in[:, f, b * P:(b + 1) * P],
                                 bd[:, 0:P:64])
                ins.then_inc(s_bonps, 1)
                keep_clock(2048, 2)
                pe.wait_ge(s_bon, l + 1)
                pe.wait_ge(s_prep, 5 * l + 5)
                step0 = NB * l
                for n, b0 in SCAN:
                    with pe.Fori(0, n) as i:
                        it = i + step0
                        keep_clock(0, 3)
                        for g in range(2):
                            r, o = G[g], g * 2048
                            pe.wait_ge(s_AR[g], 1 + it + 1)
                            pe.wait_ge(s_BK[g], 1 + it + 1)
                            pe.wait_ge(s_ye[g], 1 + it)
                            pe.wait_ge(s_Sn[g], 1 + it * 2)
                            for f in range(2):
                                ins = mm(ps[:, o + 512 * f:o + 512 * f + 512], r["bt"][:, f, :],
                                         r["ar"][:, 2 * f:2 * f + 2, :, :].rearrange("p h j t -> p (h j t)"))
                            ins.then_inc(s_pre[g], 1)
                            for f in range(2):
                                ins = mm(ps[:, o + 1024 + 512 * f:o + 1536 + 512 * f], r["kt"][:, f, :],
                                         r["ar"][:, 2 * f:2 * f + 2, :, :].rearrange("p h j t -> p (h j t)"))
                            ins.then_inc(s_pre[g], 1)
                        for g in range(2):
                            r, o = G[g], g * 2048
                            pe.wait_ge(s_msk[g], it * 3 + 1)
                            for j, src in enumerate([r["ar"][:, h, 0, :] for h in range(4)] +
                                                    [r[x][:, f, :] for x in ("bt", "kt") for f in range(2)]):
                                ins = pe.transpose(ps[:, o + j * P:o + (j + 1) * P], src, ident)
                            ins.then_inc(s_pre[g], 1)
                            pe.wait_ge(s_msk[g], it * 3 + 2)
                            for h, f, rows in HEADS:
                                ins = mm(ps[:, o + 1024 + P * h:o + 1024 + P * (h + 1)], r["ar"][:, h, 0, :], r["bt"][:, f, :])
                            ins.then_inc(s_pre[g], 1)
                        last = len(LEVELS) - 1
                        for j in range(last + 1):
                            for g in range(2):
                                r, o = G[g], g * 2048
                                if j == 0:
                                    pe.wait_ge(s_msk[g], it * 3 + 3)
                                    pe.wait_ge(s_tti[g], it + 1)
                                else:
                                    pe.wait_ge(s_Tu[g], it * 5 + j)
                                for h, f, rows in HEADS:
                                    ins = mm(ps[:, o + 1536 + P * h:o + 1536 + P * (h + 1)], r["abr"][:, h, 0:P],
                                             r["t"][:, h, :])
                                ins.then_inc(s_X[g], 1)
                                if j:
                                    for h, f, rows in HEADS:
                                        ins = pe.transpose(ps[:, o + 512 + P * h:o + 512 + P * (h + 1)],
                                                           r["t"][:, h, :], ident)
                                    ins.then_inc(s_Tt[g], 1)
                            for g in range(2):
                                r, o = G[g], g * 2048
                                pe.wait_ge(s_Xm[g], it * 5 + (j + 1))
                                if j == 0:
                                    pe.wait_ge(s_tok[g], it + 1)
                                else:
                                    pe.wait_ge(s_Tte[g], it * 4 + j)
                                for h, f, rows in HEADS:
                                    if j < last:
                                        ins = mm(ps[:, o + P * h:o + P * (h + 1)], r["tt"][:, h, :], r["x"][:, h, :])
                                    else:
                                        ins = mm(ps[:, o + 512 + P * h:o + 512 + P * (h + 1)], r["x"][:, h, :],
                                                 r["tt"][:, h, :])
                                ins.then_inc(s_Tp[g], 1)
                        for g in range(2):
                            r, o = G[g], g * 2048
                            pe.wait_ge(s_V[g], it + 1)
                            for h, f, rows in HEADS:
                                ins = mm(ps[:, o + 1536 + P * h:o + 1536 + P * (h + 1)], r["akr"][:, h, 0:P],
                                         r["vs"][:, f * P:(f + 1) * P])
                            ins.then_inc(s_kv[g], 1)
                        for g in range(2):
                            r, o = G[g], g * 2048
                            pe.wait_ge(s_Tu[g], it * 5 + 5)
                            for h, f, rows in HEADS:
                                ins = mm(ps[:, o + 1024 + P * h:o + 1024 + P * (h + 1)], r["tok"][:, P * h:P * (h + 1)],
                                         r["tt"][:, h, :])
                            ins.then_inc(s_W[g], 1)
                            pe.wait_ge(s_kve[g], it * 2 + 1)
                            for h, f, rows in HEADS:
                                ins = mm(ps[:, o + P * h:o + P * (h + 1)], r["tt"][:, h, :],
                                         r["akv"][:, 2 * f:2 * f + 2, :].rearrange("p h i -> p (h i)"))
                            ins.then_inc(s_kv[g], 1)
                        for k in range(2):
                            for g in range(2):
                                r, o = G[g], g * 2048
                                if k == 0:
                                    pe.wait_ge(s_Wt[g], it + 1)
                                    pe.wait_ge(s_kve[g], it * 2 + 2)
                                pe.wait_ge(s_Sn[g], 1 + it * 2 + k)
                                pe.wait_ge(s_Us[g], 1 + it * 2 + k)
                                c = k if g == 0 else 1 - k
                                tr = slice(64 * c, 64 * c + 64)
                                for h, f, rows in HEADS:
                                    ins = mm(ps[tr, o + 512 + P * h:o + 512 + P * (h + 1)], r["wt"][:, h, tr],
                                             st[g][:, f, :, :].rearrange("p s i -> p (s i)"))
                                ins.then_inc(s_U[g], 1)
                            for g in range(2):
                                r, o = G[g], g * 2048
                                c = k if g == 0 else 1 - k
                                tr = slice(64 * c, 64 * c + 64)
                                pe.wait_ge(s_Us[g], 1 + it * 2 + (k + 1))
                                pe.sem_inc(s_seen, 1)
                                for h, f, rows in HEADS:
                                    out = ps[rows, o + 1536 + 64 * f:o + 1600 + 64 * f]
                                    mm(out, r["tok"][tr, 768 + 64 * h:832 + 64 * h], r["vs"][tr, 64 * h:64 * h + 64], True, False)
                                    ins = mm(out, r["tok"][tr, 512 + 64 * h:576 + 64 * h], r["u"][tr, h, :], False, True)
                                ins.then_inc(s_dS[g], 1)
                        for g in range(2):
                            r, o = G[g], g * 2048
                            for h, f, rows in HEADS:
                                out = ps[:, o + 1024 + P * h:o + 1024 + P * (h + 1)]
                                two = [P, 2, 64]
                                mm(out, r["ar"][:, h, 1, :], st[g][:, f, :, :].rearrange("p s i -> p (s i)"), True, False)
                                mm(out, r["abr"][:, h, P:256], r["u"][:, h, :].unsqueeze(1).to_broadcast(two), False, False)
                                ins = mm(out, r["akr"][:, h, P:256],
                                         r["vs"][:, 64 * h:64 * h + 64].unsqueeze(1).to_broadcast(two), False, True)
                            ins.then_inc(s_y[g], 1)
                    step0 = step0 + n
                keep_clock(0, 20 if l < DEPTH - 1 else 14)
                pe.wait_ge(s_rout, 2 * (l + 1))
                for g in range(2):
                    pe.wait_ge(s_Sn[g], 1 + 2 * NB * (l + 1))
                for f in range(KT):
                    if f >= 2:
                        pe.wait_ge(s_otl, KT * l + f - 1)
                    for b in range(nbk):
                        ins = pe.transpose(ps[:, (f % 2) * 1024 + b * P:(f % 2) * 1024 + (b + 1) * P],
                                           mix[:, b, f * P:(f + 1) * P], ident)
                    ins.then_inc(s_ot, 1)
                pe.wait_ge(s_otl, KT * (l + 1))
                with pe.Fori(0, KT // SLOTS) as i:
                    for q in range(SLOTS):
                        pe.wait_ge(s_ev, 1 + i * SLOTS + (60 * l + NZ + q - 1))
                        product(o_hi, o_lo, (q % 2) * 1024, q, i + fills[0], t).then_inc(s_tile[q], 1)
                fills[0] += KT // SLOTS
                ssq(l, 1)
                keep_clock(0, 22 if l < DEPTH - 1 else 15)
                ssq(l, 2)
                with pe.Fori(0, FFG) as i:
                    for k in range(KT):
                        q = k % SLOTS
                        pe.wait_ge(s_ev, 1 + i * KT + (60 * l + NZ + KT + k - 1))
                        product(pre_hi[2], pre_lo, (k % 2) * 1024, q, i * 4 + (fills[0] + k // SLOTS), t,
                                (s_hlo, 16 * l + 9) if k == 0 else None).then_inc(s_tile[q], 1)
                    for k in range(KT):
                        q = k % SLOTS
                        if k >= 2:
                            pe.wait_ge(s_ev2, 1 + i * KT + (32 * l + k - 1))
                        else:
                            pe.wait_ge(s_ev2, 1 + i * KT + 32 * l)
                        product(h1_hi, h1_lo, 2048 + (k % 2) * 1024, q, i * 4 + (fills[0] + 2 + k // SLOTS), t,
                                (s_h1, i * KT + (32 * l + 2)) if k == 0 else None).then_inc(s_tile[q], 1)
                fills[0] += 4 * FFG
                ssq(l, 3)


def constants():
    kf = np.zeros((NKF, P, P), np.float32)
    kf[K_ID] = np.eye(P)
    kf[K_ONES] = 1.0
    kf[K_BD, 0:64, 0:64] = kf[K_BD, 64:, 64:] = 1.0
    inv = {d: (np.float32(10000.0) ** (-np.arange(d // 4, dtype=np.float32) / np.float32(d // 4))).astype(np.float32)
           for d in (64, 32)}
    t = np.arange(LAT)
    place = ((t // 64).astype(np.float32), (t % 64).astype(np.float32))

    def rotation(dim, base, size, matrix, cos, sin):
        n = dim // 4
        for part in range(2):
            ang = place[part][None, :] * inv[dim][:, None]
            for half in range(2):
                at = base + part * 2 * n + half * n
                other = base + part * 2 * n + (1 - half) * n
                cos[at:at + n] = np.cos(ang)
                sin[at:at + n] = np.sin(ang)
                for j in range(n):
                    matrix[other + j, at + j] = -1.0 if half == 0 else 1.0

    rope = np.zeros((4, P, LAT), np.float32)
    rope[2] = 1.0
    for base in (0, 64):
        rotation(64, base, P, kf[K_ROT64], rope[0], rope[1])
    rotation(32, 64, 96, kf[K_ROT96], rope[2], rope[3])

    row, col = np.arange(P)[:, None], np.arange(P)[None, :]
    same = (row // CH) == (col // CH)
    km = []
    for g in range(2):
        before = (lambda a, b: a < b) if g == 0 else (lambda a, b: a > b)
        km.append(same & before(row, col))
        km.append(same & (before(row, col) | (row == col)))
        first = (row // 2 == col // 2) & before(col, row)
        km += [first, first.T]
        for h in LEVELS:
            km.append((row // (2 * h) == col // (2 * h)) & (row // h != col // h) & before(col, row))
    km = np.stack(km).astype(np.float32)

    wmask = np.full((NBL, P, 384), NEG, np.float32)
    key = np.arange(384)[None, :] - P
    for b in range(NBL):
        at = b * P + key
        wmask[b][(np.abs(row - key) <= P) & (at >= 0) & (at < LAT)] = 0.0
    smask = np.ones((P, TOK), np.float32)
    smask[:, ::CH] = 0.0
    return (kf.transpose(1, 0, 2).reshape(P, -1), km.transpose(1, 0, 2).reshape(P, -1),
            rope.transpose(1, 0, 2), wmask.transpose(1, 0, 2), smask)


def kernel(**inputs):
    import concourse.bacc as bacc
    from concourse.bass_utils import run_bass_kernel_spmd

    a = {k: np.asarray(v) for k, v in inputs.items()}
    L = DEPTH

    def tiles(v):
        return v.reshape(L, -1, P).transpose(0, 2, 1)

    def slabs(w):
        n = w.shape[2] // P
        return w.reshape(L, KT, P, n, P).transpose(0, 3, 2, 1, 4).reshape(L * n, P, KT * P)

    ga, gb, gc, gd = 0, 512, 928, 1984
    heads = lambda at: [np.arange(at + (2 * g + r) * 64, at + (2 * g + r) * 64 + 64) for r in range(2) for g in range(2)]
    cols = [*heads(ga), np.arange(ga + 256, ga + 512), *heads(gd), np.arange(gd + 256, gd + 512),
            np.arange(gb, gb + 384), np.arange(gc, gc + 1024), np.arange(gc + 1024, gc + 1056), np.full(32, -1),
            np.arange(gb + 384, gb + 416), np.full(32, -1)]
    cols = np.concatenate(cols)
    w_in = np.concatenate([a["w_in"], np.zeros((L, DM, 1), np.float32)], axis=2)[:, :, cols]
    mu = np.concatenate([a["rwkv_mu"], np.zeros((L, 96), np.float32)], axis=1)
    mod = a["w_mod"].reshape(L, SLOTS, 2, P, 12, 512).transpose(0, 4, 1, 3, 2, 5).reshape(L * NMOD, P, 1024)
    pcol = np.concatenate([
        tiles(a["b_mod"]), tiles(a["g_pre_mix"]), tiles(a["g_post_mix"]), tiles(a["g_pre_mlp"]), tiles(a["g_post_mlp"]),
        tiles(np.tile(a["gqa_q_norm"], (1, 2))), tiles(np.tile(a["gqa_k_norm"], (1, 2))), tiles(a["mla_q_norm"]),
        tiles(a["mla_kv_norm"]), tiles(mu), tiles(a["rwkv_w0"].reshape(L, -1)), tiles(a["rwkv_a0"].reshape(L, -1)),
        tiles(a["rwkv_k_k"].reshape(L, -1)), tiles(a["rwkv_k_a"].reshape(L, -1)), tiles(a["rwkv_r_k"].reshape(L, -1)),
        np.broadcast_to(a["swa_sink"][:, None, :], (L, P, 4))], axis=2)
    kf, km, rope, wmask, smask = constants()
    g2 = np.zeros((L, P, 512), np.float32)
    g2[:, :, 0:256] = a["rwkv_g2"][:, 0:P]
    g2[:, 0:32, 256:512] = a["rwkv_g2"][:, P:160]
    w2a2 = np.zeros((L, P, 1024), np.float32)
    w2a2[:, 0:64, 0:512] = a["rwkv_w2"].transpose(0, 2, 1, 3).reshape(L, 64, 512)
    w2a2[:, 64:P, 512:1024] = a["rwkv_a2"].transpose(0, 2, 1, 3).reshape(L, 64, 512)
    tokens = np.concatenate([a["x"][0], a["ctx"][0]], axis=0)
    data = {
        "xT": tokens.T.reshape(KT, P, TOK).transpose(1, 0, 2),
        "cT": np.stack([a["c"][0], a["c_ctx"]], axis=1).reshape(KT, P, 2).transpose(1, 0, 2).reshape(P, KT * 2),
        "pcol": pcol, "constf": kf, "constm": km, "rope": rope, "wmask": wmask,
        "wmod": mod, "win": slabs(w_in), "wout": slabs(a["w_out"]), "w1": slabs(a["w_mlp1"]),
        "w2": a["w_mlp2"].reshape(L, FFG, KT, P, KT, P).transpose(0, 1, 4, 3, 2, 5).reshape(L * FFG * KT, P, DM),
        "uq": a["mla_w_uq"].reshape(L, 2, P, 384).transpose(0, 2, 1, 3),
        "ukv": a["mla_w_ukv"], "w2a2": w2a2, "g2": g2,
        "ln": np.broadcast_to(np.concatenate([a["rwkv_ln_w"], a["rwkv_ln_b"]], axis=1)[:, None, :], (L, P, 512)),
        "smask": smask,
    }
    data = {k: np.ascontiguousarray(v) for k, v in data.items()}
    nc = bacc.Bacc("TRN2", target_bir_lowering=False, num_devices=1)
    args = [nc.dram_tensor(f"{k}_dram", v.shape, mybir.dt.from_np(v.dtype), kind="ExternalInput").ap() for k, v in data.items()]
    args.append(nc.dram_tensor("out_dram", (P, KT, LAT), F32, kind="ExternalOutput").ap())
    backbone(nc, *args)
    r = run_bass_kernel_spmd(nc, [{f"{k}_dram": v for k, v in data.items()}], core_ids=[0])
    got = r.results[0]["out_dram"]
    return got.transpose(1, 0, 2).reshape(DM, LAT).T.reshape(1, LAT, DM)
```
